# Optimizing a Trainium2 kernel written in Bass

```python
import math
import jax
import jax.numpy as jnp
from jax import lax
import numpy as np

D_MODEL = 2048
BATCH = 1
SEQ = 256
DEPTH = 2

D_MIX = D_MODEL
N_GROUPS = 4
GROUP_W = D_MIX // N_GROUPS
HEAD_DIM = 128
N_HEADS = GROUP_W // HEAD_DIM
DIFF_QK_DIM = HEAD_DIM // 2
MOBA_BLOCK = 256
MOBA_TOPK = 3
MOBA_Q_CHUNK = 64
GLA_DK = HEAD_DIM // 2
GLA_DV = HEAD_DIM
GLA_RANK = 16
GLA_TAU = 16.0
GLA_CHUNK = 64
Q_BLOCK = 128
ROPE_THETA = 500000.0
ROPE_FRACTION = 4
RMS_EPS = 1e-6
FOX_F_BIAS_CENTER = 3.0

SEGMENTS = (
    ("fox_q", GROUP_W), ("fox_k", GROUP_W), ("fox_v", GROUP_W),
    ("fox_f", N_HEADS), ("fox_g", GROUP_W),
    ("diff_q", GROUP_W), ("diff_k", GROUP_W), ("diff_v", GROUP_W), ("diff_g", GROUP_W),
    ("moba_q", GROUP_W), ("moba_k", GROUP_W), ("moba_v", GROUP_W), ("moba_g", GROUP_W),
    ("gla_q", N_HEADS * GLA_DK), ("gla_k", N_HEADS * GLA_DK), ("gla_v", N_HEADS * GLA_DV),
    ("gla_a", GLA_RANK), ("gla_g", GROUP_W),
)
D_IN = sum(w for _, w in SEGMENTS)


def rms_norm(x, g):
    xf = x.astype(jnp.float32)
    y = xf * lax.rsqrt(jnp.mean(xf * xf, axis=-1, keepdims=True) + RMS_EPS)
    return (y * g.astype(jnp.float32)).astype(x.dtype)

def split_columns(proj):
    parts, off = {}, 0
    for name, width in SEGMENTS:
        parts[name] = proj[..., off:off + width]
        off += width
    return parts

def to_heads(t, d):
    b, s, _ = t.shape
    return t.reshape(b, s, -1, d).transpose(0, 2, 1, 3)

def from_heads(t):
    b, h, s, d = t.shape
    return t.transpose(0, 2, 1, 3).reshape(b, s, h * d)

def diff_pair(t):
    b, s, _ = t.shape
    t = t.reshape(b, s, N_HEADS, 2, DIFF_QK_DIM).transpose(3, 0, 2, 1, 4)
    return t[0], t[1]

def query_blocks(t, block):
    b, h, s, d = t.shape
    return t.reshape(b, h, s // block, block, d).transpose(2, 0, 1, 3, 4)

def merge_query_blocks(o):
    n, b, h, blk, d = o.shape
    return o.transpose(1, 2, 0, 3, 4).reshape(b, h, n * blk, d)

def rope_table(seq, rot_dim):
    inv_freq = ROPE_THETA ** (-jnp.arange(0, rot_dim, 2, dtype=jnp.float32) / rot_dim)
    ang = jnp.arange(seq, dtype=jnp.float32)[:, None] * inv_freq[None, :]
    return jnp.cos(ang), jnp.sin(ang)

def partial_rope(t, cos, sin):
    half = cos.shape[-1]
    rot = 2 * half
    t1, t2, rest = t[..., :half], t[..., half:rot], t[..., rot:]
    c = cos.astype(t.dtype)
    s = sin.astype(t.dtype)
    return jnp.concatenate([t1 * c - t2 * s, t1 * s + t2 * c, rest], axis=-1)

def forgetting_attention(q, k, v, log_f):
    b, h, s_len, d = q.shape
    cum = jnp.cumsum(log_f.astype(jnp.float32), axis=-1)
    n_blk = s_len // Q_BLOCK
    cum_blocks = cum.reshape(b, h, n_blk, Q_BLOCK).transpose(2, 0, 1, 3)
    k_pos = jnp.arange(s_len)
    scale = d ** -0.5

    def block(args):
        i, q_i, c_i = args
        logits = jnp.einsum("bhqd,bhkd->bhqk", q_i, k, preferred_element_type=jnp.float32) * scale
        logits = logits + c_i[..., :, None] - cum[:, :, None, :]
        q_pos = i * Q_BLOCK + jnp.arange(Q_BLOCK)
        logits = jnp.where(k_pos[None, :] <= q_pos[:, None], logits, -jnp.inf)
        p = jax.nn.softmax(logits, axis=-1)
        return jnp.einsum("bhqk,bhkd->bhqd", p.astype(v.dtype), v)

    out = lax.map(block, (jnp.arange(n_blk), query_blocks(q, Q_BLOCK), cum_blocks))
    return merge_query_blocks(out)

def differential_attention(q1, q2, k1, k2, v, lam):
    s_len, d = q1.shape[2], q1.shape[3]
    n_blk = s_len // Q_BLOCK
    k_pos = jnp.arange(s_len)
    scale = d ** -0.5

    def block(args):
        i, q1_i, q2_i = args
        q_pos = i * Q_BLOCK + jnp.arange(Q_BLOCK)
        causal = k_pos[None, :] <= q_pos[:, None]

        def probs(q_i, k_full):
            logits = jnp.einsum("bhqd,bhkd->bhqk", q_i, k_full, preferred_element_type=jnp.float32) * scale
            return jax.nn.softmax(jnp.where(causal, logits, -jnp.inf), axis=-1)

        p = probs(q1_i, k1) - lam * probs(q2_i, k2)
        return jnp.einsum("bhqk,bhkd->bhqd", p.astype(v.dtype), v)

    out = lax.map(block, (jnp.arange(n_blk), query_blocks(q1, Q_BLOCK), query_blocks(q2, Q_BLOCK)))
    return merge_query_blocks(out)

def moba_attention(q, k, v):
    b, h, s_len, d = q.shape
    n_blk = -(-s_len // MOBA_BLOCK)
    pad = n_blk * MOBA_BLOCK - s_len
    widths = ((0, 0), (0, 0), (0, pad), (0, 0))
    qp, kp, vp = (jnp.pad(t, widths) for t in (q, k, v))
    k_blocks = kp.reshape(b, h, n_blk, MOBA_BLOCK, d)
    v_blocks = vp.reshape(b, h, n_blk, MOBA_BLOCK, d)
    k_mean = jnp.mean(k_blocks.astype(jnp.float32), axis=3)
    n_sel = min(MOBA_TOPK, n_blk)
    scale = d ** -0.5
    gather = jax.vmap(jax.vmap(lambda blocks, idx: blocks[idx]))

    def chunk(args):
        c, q_c = args
        q_pos = c * MOBA_Q_CHUNK + jnp.arange(MOBA_Q_CHUNK)
        own = (c * MOBA_Q_CHUNK) // MOBA_BLOCK
        gate = jnp.einsum("bhqd,bhnd->bhqn", q_c.astype(jnp.float32), k_mean)
        gate = jnp.where(jnp.arange(n_blk) < own, gate, -jnp.inf)
        _, top_idx = lax.top_k(gate, n_sel)
        sel_ok = jnp.arange(n_sel) < own
        k_sel = gather(k_blocks, top_idx)
        v_sel = gather(v_blocks, top_idx)
        s_sel = jnp.einsum("bhqd,bhqjld->bhqjl", q_c, k_sel, preferred_element_type=jnp.float32) * scale
        s_sel = jnp.where(sel_ok[:, None], s_sel, -jnp.inf).reshape(b, h, MOBA_Q_CHUNK, n_sel * MOBA_BLOCK)
        k_own = lax.dynamic_slice_in_dim(kp, own * MOBA_BLOCK, MOBA_BLOCK, axis=2)
        v_own = lax.dynamic_slice_in_dim(vp, own * MOBA_BLOCK, MOBA_BLOCK, axis=2)
        s_own = jnp.einsum("bhqd,bhld->bhql", q_c, k_own, preferred_element_type=jnp.float32) * scale
        own_pos = own * MOBA_BLOCK + jnp.arange(MOBA_BLOCK)
        s_own = jnp.where(own_pos[None, :] <= q_pos[:, None], s_own, -jnp.inf)
        p = jax.nn.softmax(jnp.concatenate([s_sel, s_own], axis=-1), axis=-1).astype(v.dtype)
        p_sel = p[..., :n_sel * MOBA_BLOCK].reshape(b, h, MOBA_Q_CHUNK, n_sel, MOBA_BLOCK)
        p_own = p[..., n_sel * MOBA_BLOCK:]
        return (jnp.einsum("bhqjl,bhqjld->bhqd", p_sel, v_sel)
                + jnp.einsum("bhql,bhld->bhqd", p_own, v_own))

    n_chunk = (n_blk * MOBA_BLOCK) // MOBA_Q_CHUNK
    out = lax.map(chunk, (jnp.arange(n_chunk), query_blocks(qp, MOBA_Q_CHUNK)))
    return merge_query_blocks(out)[:, :, :s_len]

def gla_chunked(q, k, v, log_a):
    b, h, s_len, dk = q.shape
    dv = v.shape[-1]
    qf = q.astype(jnp.float32) * dk ** -0.5
    kf = k.astype(jnp.float32)
    vf = v.astype(jnp.float32)
    gf = log_a.astype(jnp.float32)
    qc, kc, vc, gc = (query_blocks(t, GLA_CHUNK) for t in (qf, kf, vf, gf))
    causal = jnp.tril(jnp.ones((GLA_CHUNK, GLA_CHUNK), dtype=bool))[..., None]

    def step(state, inp):
        q_i, k_i, v_i, g_i = inp
        cum = jnp.cumsum(g_i, axis=2)
        rel = jnp.where(causal, cum[:, :, :, None, :] - cum[:, :, None, :, :], -jnp.inf)
        scores = jnp.einsum("bhtd,bhsd,bhtsd->bhts", q_i, k_i, jnp.exp(rel))
        o = (jnp.einsum("bhts,bhsv->bhtv", scores, v_i)
             + jnp.einsum("bhtd,bhdv->bhtv", q_i * jnp.exp(cum), state))
        last = cum[:, :, -1:, :]
        state = (jnp.exp(last[:, :, 0, :])[..., None] * state
                 + jnp.einsum("bhsd,bhsv->bhdv", k_i * jnp.exp(last - cum), v_i))
        return state, o

    state0 = jnp.zeros((b, h, dk, dv), jnp.float32)
    _, out = lax.scan(step, state0, (qc, kc, vc, gc))
    return merge_query_blocks(out).astype(v.dtype)

def hybrid_layer(x, layer_idx, norm_g, w_in, fox_fb, diff_lam, diff_norm_g,
                 gla_wa2, gla_ba, gla_norm_g, w_out, rope_diff, rope_moba):
    h = rms_norm(x, norm_g)
    p = split_columns(jnp.einsum("bsd,de->bse", h, w_in))

    log_f = jax.nn.log_sigmoid((p["fox_f"] + fox_fb).astype(jnp.float32)).transpose(0, 2, 1)
    fox = forgetting_attention(to_heads(p["fox_q"], HEAD_DIM), to_heads(p["fox_k"], HEAD_DIM),
                               to_heads(p["fox_v"], HEAD_DIM), log_f)
    fox = from_heads(fox) * jax.nn.silu(p["fox_g"])

    lambda_init = 0.8 - 0.6 * math.exp(-0.3 * layer_idx)
    lf = diff_lam.astype(jnp.float32)
    lam = jnp.exp(jnp.sum(lf[0] * lf[1])) - jnp.exp(jnp.sum(lf[2] * lf[3])) + lambda_init
    q1, q2 = diff_pair(p["diff_q"])
    k1, k2 = diff_pair(p["diff_k"])
    q1, q2, k1, k2 = (partial_rope(t, *rope_diff) for t in (q1, q2, k1, k2))
    diff = differential_attention(q1, q2, k1, k2, to_heads(p["diff_v"], HEAD_DIM), lam)
    diff = rms_norm(diff, diff_norm_g) * (1.0 - lambda_init)
    diff = from_heads(diff) * jax.nn.silu(p["diff_g"])

    mq = partial_rope(to_heads(p["moba_q"], HEAD_DIM), *rope_moba)
    mk = partial_rope(to_heads(p["moba_k"], HEAD_DIM), *rope_moba)
    moba = moba_attention(mq, mk, to_heads(p["moba_v"], HEAD_DIM))
    moba = from_heads(moba) * jax.nn.silu(p["moba_g"])

    a_logit = jnp.einsum("bsr,re->bse", p["gla_a"], gla_wa2) + gla_ba
    log_a = jax.nn.log_sigmoid(a_logit.astype(jnp.float32)) / GLA_TAU
    gla = gla_chunked(to_heads(p["gla_q"], GLA_DK), to_heads(p["gla_k"], GLA_DK),
                      to_heads(p["gla_v"], GLA_DV), to_heads(log_a, GLA_DK))
    gla = from_heads(rms_norm(gla, gla_norm_g)) * jax.nn.silu(p["gla_g"])

    mixed = jnp.concatenate([fox, diff, moba, gla], axis=-1)
    return x + jnp.einsum("bse,ed->bsd", mixed, w_out)

def first_inputs(seed: int = 0) -> dict:
    key = jax.random.key(seed)
    ks = jax.random.split(key, 11)
    f32 = jnp.float32
    nrm = jax.random.normal
    x = nrm(ks[0], (BATCH, SEQ, D_MODEL), f32)
    norm_g = 1.0 + 0.02 * nrm(ks[1], (DEPTH, D_MODEL), f32)
    w_in = nrm(ks[2], (DEPTH, D_MODEL, D_IN), f32) * D_MODEL ** -0.5
    fox_fb = FOX_F_BIAS_CENTER + 0.1 * nrm(ks[3], (DEPTH, N_HEADS), f32)
    diff_lam = 0.1 * nrm(ks[4], (DEPTH, 4, DIFF_QK_DIM), f32)
    diff_norm_g = 1.0 + 0.02 * nrm(ks[5], (DEPTH, HEAD_DIM), f32)
    gla_wa2 = nrm(ks[6], (DEPTH, GLA_RANK, N_HEADS * GLA_DK), f32) * GLA_RANK ** -0.5
    gla_ba = 0.1 * nrm(ks[7], (DEPTH, N_HEADS * GLA_DK), f32)
    gla_norm_g = 1.0 + 0.02 * nrm(ks[8], (DEPTH, GLA_DV), f32)
    w_out = nrm(ks[9], (DEPTH, D_MIX, D_MODEL), f32) * D_MIX ** -0.5
    final_norm_g = 1.0 + 0.02 * nrm(ks[10], (D_MODEL,), f32)
    return {"x": x, "norm_g": norm_g, "w_in": w_in, "fox_fb": fox_fb, "diff_lam": diff_lam,
            "diff_norm_g": diff_norm_g, "gla_wa2": gla_wa2, "gla_ba": gla_ba,
            "gla_norm_g": gla_norm_g, "w_out": w_out, "final_norm_g": final_norm_g}

def first_block(x, norm_g, w_in, fox_fb, diff_lam, diff_norm_g, gla_wa2, gla_ba,
              gla_norm_g, w_out, final_norm_g):
    s_len = x.shape[1]
    rope_diff = rope_table(s_len, DIFF_QK_DIM // ROPE_FRACTION)
    rope_moba = rope_table(s_len, HEAD_DIM // ROPE_FRACTION)
    for l in range(DEPTH):
        x = hybrid_layer(x, l, norm_g[l], w_in[l], fox_fb[l], diff_lam[l], diff_norm_g[l],
                         gla_wa2[l], gla_ba[l], gla_norm_g[l], w_out[l], rope_diff, rope_moba)
    return rms_norm(x, final_norm_g)


DEPTH_2 = 1

CTX_LEN = 256
GRID_W = 64

A_WIDTH = D_MODEL // 2
A_HEAD = 64
A_HEADS = A_WIDTH // A_HEAD
A_DECAY_LORA = 96
A_ICLR_LORA = 128
A_GATE_LORA = 256
A_GN_EPS = 64e-5

B_WIDTH = D_MODEL // 2
B_HEAD = 128
B_HEADS = B_WIDTH // B_HEAD
B_CONV = 3
B_CHUNK = 64

D_FF = 4 * D_MODEL

A_COLS = 3 * A_WIDTH + A_DECAY_LORA + A_ICLR_LORA + A_GATE_LORA
B_COLS = 4 * B_WIDTH + 4 * B_HEADS
GATE_COLS = 2 * D_MODEL
IN_COLS = A_COLS + B_COLS + GATE_COLS


def split_cols(z, sizes):
    offs = np.cumsum(sizes)[:-1].tolist()
    return jnp.split(z, offs, axis=-1)

def rms_norm_2(x, w):
    xf = x.astype(jnp.float32)
    y = xf * lax.rsqrt(jnp.mean(xf * xf, axis=-1, keepdims=True) + RMS_EPS)
    return (y * w.astype(jnp.float32)).astype(x.dtype)

def l2_normalize(z):
    return z * lax.rsqrt(jnp.sum(z * z, axis=-1, keepdims=True) + 1e-12)

def modulate(h, shift, scale):
    return h * (1.0 + scale) + shift

def grid_shift(z):
    bsz, t, c = z.shape
    g = z.reshape(bsz, t // GRID_W, GRID_W, c // 4, 4)
    zero_col = jnp.zeros_like(g[:, :, :1, :, 0])
    zero_row = jnp.zeros_like(g[:, :1, :, :, 0])
    left = jnp.concatenate([zero_col, g[:, :, :-1, :, 0]], axis=2)
    right = jnp.concatenate([g[:, :, 1:, :, 1], zero_col], axis=2)
    up = jnp.concatenate([zero_row, g[:, :-1, :, :, 2]], axis=1)
    down = jnp.concatenate([g[:, 1:, :, :, 3], zero_row], axis=1)
    return jnp.stack([left, right, up, down], axis=-1).reshape(bsz, t, c)

def seq_shift(z):
    bsz, t, c = z.shape
    g = z.reshape(bsz, t, c // 2, 2)
    zero = jnp.zeros_like(g[:, :1, :, 0])
    prev = jnp.concatenate([zero, g[:, :-1, :, 0]], axis=1)
    nxt = jnp.concatenate([g[:, 1:, :, 1], zero], axis=1)
    return jnp.stack([prev, nxt], axis=-1).reshape(bsz, t, c)

def centred_conv(z, w):
    k = w.shape[0]
    return lax.conv_general_dilated(
        z, w.astype(z.dtype)[:, None, :], window_strides=(1,),
        padding=[((k - 1) // 2, k // 2)], dimension_numbers=('NWC', 'WIO', 'NWC'),
        feature_group_count=z.shape[-1])

def rwkv7_prepare(z, w0, w_up, a0, a_up, k_k, k_a):
    bsz, t, _ = z.shape
    heads = lambda u: u.reshape(bsz, t, A_HEADS, A_HEAD)
    r, k, v, xw, xa, xg = split_cols(z, [A_WIDTH] * 3 + [A_DECAY_LORA, A_ICLR_LORA, A_GATE_LORA])
    kk = l2_normalize(heads(k * k_k))
    tw = jnp.tanh(xw)
    dirs = []
    for d in range(2):
        w = -jax.nn.softplus(-(w0[d] + tw @ w_up[d])) - 0.5
        a = jax.nn.sigmoid(a0[d] + xa @ a_up[d])
        k_d = k * (1.0 + (a - 1.0) * k_a)
        dirs.append((heads(jnp.exp(-jnp.exp(w))), heads(k_d), heads(a) * kk))
    return heads(r), heads(v), kk, xg, dirs

def rwkv7_scan(r, decay, k, v, kk, b, s0, reverse, with_out):
    seq = (decay, k, v, kk, b) + ((r,) if with_out else ())
    xs = tuple(jnp.swapaxes(u, 0, 1) for u in seq)

    def step(s, inp):
        dec_t, k_t, v_t, kk_t, b_t = inp[:5]
        sa = jnp.einsum('bhvk,bhk->bhv', s, kk_t)
        s = (s * dec_t[:, :, None, :] - sa[..., None] * b_t[:, :, None, :]
             + v_t[..., None] * k_t[:, :, None, :])
        if with_out:
            return s, jnp.einsum('bhvk,bhk->bhv', s, inp[5])
        return s, None

    s, ys = lax.scan(step, s0, xs, reverse=reverse)
    return (jnp.swapaxes(ys, 0, 1) if with_out else None), s

def rwkv7_readout(y, r, k_dirs, v, xg, g_up, r_k, ln_w, ln_b):
    bsz, t = y.shape[:2]
    mean = jnp.mean(y, axis=-1, keepdims=True)
    var = jnp.mean(jnp.square(y - mean), axis=-1, keepdims=True)
    yn = ((y - mean) * lax.rsqrt(var + A_GN_EPS)).reshape(bsz, t, A_WIDTH) * ln_w + ln_b
    bonus = sum(jnp.sum(r * k_d * r_k, axis=-1, keepdims=True) for k_d in k_dirs) * v
    gate = jax.nn.sigmoid(xg) @ g_up
    return (yn + bonus.reshape(bsz, t, A_WIDTH)) * gate

def rwkv7_branch(za, za_ctx, mu, w0, w_up, a0, a_up, g_up, k_k, k_a, r_k, ln_w, ln_b, ctx_out):
    za = za + (grid_shift(za) - za) * mu
    za_ctx = za_ctx + (seq_shift(za_ctx) - za_ctx) * mu
    r, v, kk, xg, dirs = rwkv7_prepare(za, w0, w_up, a0, a_up, k_k, k_a)
    rc, vc, kkc, xgc, dirs_c = rwkv7_prepare(za_ctx, w0, w_up, a0, a_up, k_k, k_a)
    s0 = jnp.zeros((za.shape[0], A_HEADS, A_HEAD, A_HEAD), jnp.float32)
    ys, ys_c = [], []
    for d in range(2):
        rev = d == 1
        dec_c, k_c, b_c = dirs_c[d]
        y_c, s_ctx = rwkv7_scan(rc, dec_c, k_c, vc, kkc, b_c, s0, rev, ctx_out)
        dec, k_d, b = dirs[d]
        y_d, _ = rwkv7_scan(r, dec, k_d, v, kk, b, s_ctx, rev, True)
        ys.append(y_d)
        ys_c.append(y_c)
    out = rwkv7_readout(ys[0] + ys[1], r, [dirs[0][1], dirs[1][1]], v, xg, g_up, r_k, ln_w, ln_b)
    out_c = None
    if ctx_out:
        out_c = rwkv7_readout(ys_c[0] + ys_c[1], rc, [dirs_c[0][1], dirs_c[1][1]], vc, xgc,
                              g_up, r_k, ln_w, ln_b)
    return out, out_c

def gdn_prepare(z, conv_w, a_log, dt_bias):
    bsz, t, _ = z.shape
    qkv, gz, a_cols, b_cols = split_cols(z, [3 * B_WIDTH, B_WIDTH, 2 * B_HEADS, 2 * B_HEADS])
    qkv = jax.nn.silu(centred_conv(qkv, conv_w))
    heads = lambda u: u.reshape(bsz, t, B_HEADS, B_HEAD)
    q, k, v = (heads(u) for u in jnp.split(qkv, 3, axis=-1))
    q = l2_normalize(q) * (B_HEAD ** -0.5)
    k = l2_normalize(k)
    g = -jnp.exp(a_log) * jax.nn.softplus(a_cols.reshape(bsz, t, 2, B_HEADS) + dt_bias)
    beta = jax.nn.sigmoid(b_cols.reshape(bsz, t, 2, B_HEADS))
    return q, k, v, g, beta, gz

def gdn_chunked(q, k, v, g, beta, s0, with_out):
    bsz, t, nh, _ = q.shape
    dv = v.shape[-1]
    nc = t // B_CHUNK
    blk = lambda u: jnp.swapaxes(u.reshape((bsz, nc, B_CHUNK) + u.shape[2:]), 2, 3)
    q, k, v, g, beta = blk(q), blk(k), blk(v), blk(g), blk(beta)
    gc = jnp.cumsum(g, axis=-1)
    idx = jnp.arange(B_CHUNK)
    incl = idx[:, None] >= idx[None, :]
    decay = jnp.exp(jnp.where(incl, gc[..., :, None] - gc[..., None, :], -jnp.inf))
    kb = k * beta[..., None]
    a_mat = jnp.einsum('bnhid,bnhjd->bnhij', kb, k) * decay
    a_mat = jnp.where(idx[:, None] > idx[None, :], a_mat, 0.0) + jnp.eye(B_CHUNK, dtype=jnp.float32)
    rhs = jnp.concatenate([v * beta[..., None], kb * jnp.exp(gc)[..., None]], axis=-1)
    sol = lax.linalg.triangular_solve(a_mat, rhs, left_side=True, lower=True, unit_diagonal=True)
    u, w = sol[..., :dv], sol[..., dv:]
    k_end = k * jnp.exp(gc[..., -1:] - gc)[..., None]
    g_end = jnp.exp(gc[..., -1])
    seq = (u, w, k_end, g_end)
    if with_out:
        attn = jnp.einsum('bnhid,bnhjd->bnhij', q, k) * decay
        seq = seq + (attn, q * jnp.exp(gc)[..., None])
    xs = tuple(jnp.moveaxis(z, 1, 0) for z in seq)

    def step(s, inp):
        u_n, w_n, k_n, g_n = inp[:4]
        v_new = u_n - jnp.einsum('bhcd,bhdv->bhcv', w_n, s)
        s_new = s * g_n[..., None, None] + jnp.einsum('bhcd,bhcv->bhdv', k_n, v_new)
        if with_out:
            attn_n, qg_n = inp[4:]
            o = jnp.einsum('bhcd,bhdv->bhcv', qg_n, s) + jnp.einsum('bhij,bhjv->bhiv', attn_n, v_new)
            return s_new, o
        return s_new, None

    s, o = lax.scan(step, s0, xs)
    if with_out:
        o = jnp.swapaxes(jnp.moveaxis(o, 0, 1), 2, 3).reshape(bsz, t, nh, dv)
    return o, s

def gdn_readout(o, gz, norm_w):
    bsz, t = o.shape[:2]
    on = o * lax.rsqrt(jnp.mean(o * o, axis=-1, keepdims=True) + RMS_EPS) * norm_w
    return (on * jax.nn.silu(gz.reshape(bsz, t, B_HEADS, B_HEAD))).reshape(bsz, t, B_WIDTH)

def gdn_branch(zb, zb_ctx, conv_w, a_log, dt_bias, norm_w, ctx_out):
    q, k, v, g, beta, gz = gdn_prepare(zb, conv_w, a_log, dt_bias)
    qc, kc, vc, gcx, betac, gzc = gdn_prepare(zb_ctx, conv_w, a_log, dt_bias)
    s0 = jnp.zeros((zb.shape[0], B_HEADS, B_HEAD, B_HEAD), jnp.float32)
    outs, outs_c = [], []
    for d in range(2):
        fl = (lambda u: u[:, ::-1]) if d == 1 else (lambda u: u)
        o_c, s_ctx = gdn_chunked(fl(qc), fl(kc), fl(vc), fl(gcx[:, :, d]), fl(betac[:, :, d]), s0, ctx_out)
        o, _ = gdn_chunked(fl(q), fl(k), fl(v), fl(g[:, :, d]), fl(beta[:, :, d]), s_ctx, True)
        outs.append(fl(o))
        if ctx_out:
            outs_c.append(fl(o_c))
    out = gdn_readout(outs[0] + outs[1], gz, norm_w)
    out_c = gdn_readout(outs_c[0] + outs_c[1], gzc, norm_w) if ctx_out else None
    return out, out_c

def merge_branches(ya, yb, pg, up_a, up_b, out_w):
    gate_a, gate_b = jnp.split(jax.nn.sigmoid(pg), 2, axis=-1)
    return (gate_a * (ya @ up_a) + gate_b * (yb @ up_b)) @ out_w

def squared_relu_mlp(h, w1, w2):
    return jnp.square(jax.nn.relu(h @ w1)) @ w2

def trunk_layer(x, ctx, c, c_ctx, mod_w, mod_b, norm1_w, norm2_w, in_w, rwkv_mu, rwkv_w0,
                rwkv_w_up, rwkv_a0, rwkv_a_up, rwkv_g_up, rwkv_k_k, rwkv_k_a, rwkv_r_k, rwkv_ln_w,
                rwkv_ln_b, gdn_conv_w, gdn_a_log, gdn_dt_bias, gdn_norm_w, up_a, up_b, out_w,
                mlp_w1, mlp_w2, last):
    dt = x.dtype
    f32 = jnp.float32
    mod = jax.nn.silu(c) @ mod_w + mod_b
    mod_c = jax.nn.silu(c_ctx) @ mod_w + mod_b
    sh1, sc1, g1, sh2, sc2, g2 = jnp.split(mod[:, None, :], 6, axis=-1)
    csh1, csc1, cg1, csh2, csc2, cg2 = jnp.split(mod_c[None, None, :], 6, axis=-1)

    h = modulate(rms_norm_2(x, norm1_w), sh1, sc1)
    hc = modulate(rms_norm_2(ctx, norm1_w), csh1, csc1)
    p = h @ in_w
    pc = hc @ (in_w[:, :A_COLS + B_COLS] if last else in_w)
    pa, pb, pg = split_cols(p, [A_COLS, B_COLS, GATE_COLS])
    pca, pcb = pc[..., :A_COLS], pc[..., A_COLS:A_COLS + B_COLS]

    ya, ya_c = rwkv7_branch(pa.astype(f32), pca.astype(f32), rwkv_mu, rwkv_w0, rwkv_w_up, rwkv_a0,
                            rwkv_a_up, rwkv_g_up, rwkv_k_k, rwkv_k_a, rwkv_r_k, rwkv_ln_w,
                            rwkv_ln_b, not last)
    yb, yb_c = gdn_branch(pb.astype(f32), pcb.astype(f32), gdn_conv_w, gdn_a_log, gdn_dt_bias,
                          gdn_norm_w, not last)

    x = x + g1 * merge_branches(ya.astype(dt), yb.astype(dt), pg, up_a, up_b, out_w)
    x = x + g2 * squared_relu_mlp(modulate(rms_norm_2(x, norm2_w), sh2, sc2), mlp_w1, mlp_w2)
    if not last:
        ctx = ctx + cg1 * merge_branches(ya_c.astype(dt), yb_c.astype(dt), pc[..., A_COLS + B_COLS:],
                                         up_a, up_b, out_w)
        ctx = ctx + cg2 * squared_relu_mlp(modulate(rms_norm_2(ctx, norm2_w), csh2, csc2), mlp_w1, mlp_w2)
    return x, ctx

def second_inputs(seed: int = 0) -> dict:
    key = jax.random.key(seed)
    ks = iter(jax.random.split(key, 40))
    nrm = lambda shape, scale: jax.random.normal(next(ks), shape, jnp.float32) * scale
    uni = lambda shape, lo, hi: jax.random.uniform(next(ks), shape, jnp.float32, lo, hi)
    L, D = DEPTH_2, D_MODEL
    dt_init = jnp.exp(uni((L, 2, B_HEADS), math.log(1e-3), math.log(1e-1)))
    return {
        'x': nrm((BATCH, SEQ, D), 1.0),
        'c': nrm((BATCH, D), 1.0),
        'ctx': nrm((BATCH, CTX_LEN, D), 1.0),
        'c_ctx': nrm((D,), 1.0),
        'mod_w': nrm((L, D, 6 * D), 0.5 * D ** -0.5),
        'mod_b': nrm((L, 6 * D), 0.02),
        'norm1_w': 1.0 + nrm((L, D), 0.1),
        'norm2_w': 1.0 + nrm((L, D), 0.1),
        'in_w': nrm((L, D, IN_COLS), D ** -0.5),
        'rwkv_mu': uni((L, A_COLS), 0.0, 1.0),
        'rwkv_w0': uni((L, 2, A_WIDTH), -3.0, 1.0),
        'rwkv_w_up': nrm((L, 2, A_DECAY_LORA, A_WIDTH), 0.5 * A_DECAY_LORA ** -0.5),
        'rwkv_a0': nrm((L, 2, A_WIDTH), 0.5),
        'rwkv_a_up': nrm((L, 2, A_ICLR_LORA, A_WIDTH), 0.5 * A_ICLR_LORA ** -0.5),
        'rwkv_g_up': nrm((L, A_GATE_LORA, A_WIDTH), A_GATE_LORA ** -0.5),
        'rwkv_k_k': 0.85 + nrm((L, A_WIDTH), 0.05),
        'rwkv_k_a': 1.0 + nrm((L, A_WIDTH), 0.05),
        'rwkv_r_k': nrm((L, A_HEADS, A_HEAD), 0.1),
        'rwkv_ln_w': 1.0 + nrm((L, A_WIDTH), 0.1),
        'rwkv_ln_b': nrm((L, A_WIDTH), 0.02),
        'gdn_conv_w': nrm((L, B_CONV, 3 * B_WIDTH), B_CONV ** -0.5),
        'gdn_a_log': jnp.log(uni((L, 2, B_HEADS), 1.0, 16.0)),
        'gdn_dt_bias': dt_init + jnp.log(-jnp.expm1(-dt_init)),
        'gdn_norm_w': 1.0 + nrm((L, B_HEAD), 0.1),
        'up_a': nrm((L, A_WIDTH, D), A_WIDTH ** -0.5),
        'up_b': nrm((L, B_WIDTH, D), B_WIDTH ** -0.5),
        'out_w': nrm((L, D, D), D ** -0.5),
        'mlp_w1': nrm((L, D, D_FF), D ** -0.5),
        'mlp_w2': nrm((L, D_FF, D), D_FF ** -0.5),
        'final_norm_w': 1.0 + nrm((D,), 0.1),
    }

def second_block(x, c, ctx, c_ctx, mod_w, mod_b, norm1_w, norm2_w, in_w, rwkv_mu, rwkv_w0, rwkv_w_up,
              rwkv_a0, rwkv_a_up, rwkv_g_up, rwkv_k_k, rwkv_k_a, rwkv_r_k, rwkv_ln_w, rwkv_ln_b,
              gdn_conv_w, gdn_a_log, gdn_dt_bias, gdn_norm_w, up_a, up_b, out_w, mlp_w1, mlp_w2,
              final_norm_w):
    for l in range(DEPTH_2):
        x, ctx = trunk_layer(
            x, ctx, c, c_ctx, mod_w[l], mod_b[l], norm1_w[l], norm2_w[l], in_w[l], rwkv_mu[l],
            rwkv_w0[l], rwkv_w_up[l], rwkv_a0[l], rwkv_a_up[l], rwkv_g_up[l], rwkv_k_k[l],
            rwkv_k_a[l], rwkv_r_k[l], rwkv_ln_w[l], rwkv_ln_b[l], gdn_conv_w[l], gdn_a_log[l],
            gdn_dt_bias[l], gdn_norm_w[l], up_a[l], up_b[l], out_w[l], mlp_w1[l], mlp_w2[l],
            last=(l == DEPTH_2 - 1))
    return rms_norm_2(x, final_norm_w)


def setup_inputs(seed=0):
    out = dict(first_inputs(seed))
    for name, value in second_inputs(seed + 1).items():
        if name != "x":
            out[name + "_2"] = value
    return out


def reference(
    x, norm_g, w_in, fox_fb, diff_lam, diff_norm_g, gla_wa2, gla_ba, gla_norm_g, w_out,
    final_norm_g, c_2, ctx_2, c_ctx_2, mod_w_2, mod_b_2, norm1_w_2, norm2_w_2, in_w_2,
    rwkv_mu_2, rwkv_w0_2, rwkv_w_up_2, rwkv_a0_2, rwkv_a_up_2, rwkv_g_up_2, rwkv_k_k_2,
    rwkv_k_a_2, rwkv_r_k_2, rwkv_ln_w_2, rwkv_ln_b_2, gdn_conv_w_2, gdn_a_log_2, gdn_dt_bias_2,
    gdn_norm_w_2, up_a_2, up_b_2, out_w_2, mlp_w1_2, mlp_w2_2, final_norm_w_2,
):
    x = first_block(
        x, norm_g, w_in, fox_fb, diff_lam, diff_norm_g, gla_wa2, gla_ba, gla_norm_g, w_out,
        final_norm_g,
    )
    return second_block(
        x, c_2, ctx_2, c_ctx_2, mod_w_2, mod_b_2, norm1_w_2, norm2_w_2, in_w_2, rwkv_mu_2,
        rwkv_w0_2, rwkv_w_up_2, rwkv_a0_2, rwkv_a_up_2, rwkv_g_up_2, rwkv_k_k_2, rwkv_k_a_2,
        rwkv_r_k_2, rwkv_ln_w_2, rwkv_ln_b_2, gdn_conv_w_2, gdn_a_log_2, gdn_dt_bias_2,
        gdn_norm_w_2, up_a_2, up_b_2, out_w_2, mlp_w1_2, mlp_w2_2, final_norm_w_2,
    )


_drawn_inputs = setup_inputs


def setup_inputs(seed=0):
    import zlib

    import numpy as np

    out = dict(_drawn_inputs(seed))
    spreads = {}
    factors = {'fox_fb': 52.304,
     'diff_norm_g': 8.0,
     'gla_ba': 3.149,
     'gla_norm_g': 6.823,
     'final_norm_g': 2.768,
     'ctx_2': 3.105,
     'c_ctx_2': 5.013,
     'rwkv_w_up_2': 8.0,
     'rwkv_a0_2': 2.951,
     'rwkv_a_up_2': 3.345,
     'rwkv_k_k_2': 64.0,
     'rwkv_k_a_2': 31.842,
     'rwkv_ln_w_2': 17.936,
     'rwkv_ln_b_2': 64.0,
     'gdn_a_log_2': 2.833,
     'gdn_norm_w_2': 16.785,
     'norm2_w_2': 3.283}
    for name, (base, spread) in spreads.items():
        noise = np.random.default_rng([zlib.crc32(name.encode()), seed]).standard_normal(out[name].shape)
        drawn = base * np.exp(spread * noise) if base else spread * noise
        out[name] = jnp.asarray(drawn.astype(out[name].dtype))
    for name, factor in factors.items():
        out[name] = (out[name] * factor).astype(out[name].dtype)
    return out
```

```python
import concourse.bass as bass
from concourse import mybir
from collections import deque
from contextlib import ExitStack
import math
import numpy as np

F32 = mybir.dt.float32
U8 = mybir.dt.uint8
ALU = mybir.AluOpType
ACT = mybir.ActivationFunctionType
AX = mybir.AxisListType

NW1 = 60
NWO = 16
NMOD = 96
NIN = 24 + 1 + 1 + 2 + 32 + 32
NT = 2 * (NW1 + NWO) + NMOD + NIN + 16 + 16 + 64 + 64
EPS = 1e-6
NSLOT = 4

PAR = {}
PARN = 0
for _n, _w in (("ng", 32), ("fb", 8), ("lam", 8), ("dng", 2), ("gng", 2), ("gba", 4), ("wa2", 512), ("fng", 16),
               ("c", 32), ("modb", 96), ("n1", 16), ("n2", 16), ("mu", 28), ("w0", 16), ("a0", 16), ("kk", 8),
               ("ka", 8), ("rk", 8), ("lnw", 8), ("lnb", 8), ("conv", 72), ("alog", 16), ("dtb", 16), ("gnw", 1),
               ("fnw", 16)):
    PAR[_n] = (PARN, _w)
    PARN += _w

CST = {}
CSTN = 0
for _n, _w in (("ident", 128), ("ones", 128), ("bones", 128), ("LE", 128), ("GT", 128), ("GE", 128), ("LT", 128),
               ("G1", 256), ("mask3", 384), ("permd", 128), ("permm", 128), ("Cd", 256), ("Sd", 256), ("Cm", 256),
               ("Sm", 256), ("scan", 512), ("type", 6), ("strict", 256), ("incl", 256)):
    CST[_n] = (CSTN, _w)
    CSTN += _w
MSK = {"strict": (0, 256), "incl": (256, 256), "lev": (512, 896), "xt0": (1408, 128), "gla": (1536, 1024)}
MSKN = 2560


def constants():
    i = np.arange(128)
    a, b = i[:, None], i[None, :]
    c = np.zeros((128, CSTN), np.float32)

    def put(name, v):
        o, w = CST[name]
        c[:, o:o + w] = v

    put("ident", a == b)
    put("ones", 1.0)
    put("bones", (a // 64) == (b // 64))
    put("LE", a <= b)
    put("GT", a > b)
    put("GE", a >= b)
    put("LT", a < b)
    put("G1", np.concatenate([np.ones((128, 128)), a > b], 1))
    tri = np.where(b > a, np.float32(-1e30), np.float32(0.0))
    put("mask3", np.concatenate([tri, np.zeros((128, 128)), tri], 1))
    t = np.arange(256, dtype=np.float32)
    for nm, rot, width, pn in (("d", 16, 64, "permd"), ("m", 32, 128, "permm")):
        half = rot // 2
        inv = (np.float32(500000.0) ** (-np.arange(0, rot, 2, dtype=np.float32) / np.float32(rot))).astype(np.float32)
        ang = t[None, :] * inv[:, None]
        C = np.ones((128, 256), np.float32)
        S = np.zeros((128, 256), np.float32)
        L = np.zeros((128, 128), np.float32)
        for base in range(0, 128, width):
            for q in range(half):
                C[base + q] = C[base + half + q] = np.cos(ang[q])
                S[base + q] = S[base + half + q] = np.sin(ang[q])
                L[base + half + q, base + q] = -1.0
                L[base + q, base + half + q] = 1.0
        put("C" + nm, C)
        put("S" + nm, S)
        put(pn, L)
    sc = np.ones(512)
    sc[::128] = 0
    put("scan", sc[None, :])
    ty = np.zeros((128, 6))
    for q in range(4):
        ty[:, q] = i % 4 == q
    for q in range(2):
        ty[:, 4 + q] = i % 2 == q
    put("type", ty)
    st = np.concatenate([a < b, a > b], 1)
    inc = np.concatenate([a <= b, a >= b], 1)
    put("strict", st)
    put("incl", inc)
    m = np.zeros((128, MSKN), np.uint8)
    m[:, 0:256] = st
    m[:, 256:512] = inc
    j = np.arange(64)
    for d in range(2):
        for lv in range(7):
            w = 1 << lv
            s = (j // w) * 2 * w + d * w + j % w
            ok = (i[:, None] // (2 * w) == s[None, :] // (2 * w)) & ((i[:, None] // w) % 2 != (s[None, :] // w) % 2)
            m[:, 512 + (d * 7 + lv) * 64:512 + (d * 7 + lv) * 64 + 64] = ok
        tcol = 2 * j + 1 - d
        m[:, 1408 + d * 64:1408 + d * 64 + 64] = (i[:, None] // 2 == tcol[None, :] // 2) & (i[:, None] != tcol[None, :])
    for lv in range(7):
        w = 1 << lv
        m[:, 1536 + lv * 128:1536 + lv * 128 + 128] = (a // (2 * w) == b // (2 * w)) & ((a // w) % 2 == 0) & ((b // w) % 2 == 1)
    m[:, 1536 + 896:1536 + 1024] = a == b
    return c, m


class Tok:
    __slots__ = ("sem", "val", "need", "inc")

    def __init__(self, sem, inc=1):
        self.sem, self.val, self.need, self.inc = sem, None, False, inc


class Queues:

    def __init__(self):
        self.ops = {k: [] for k in ("t", "v", "a", "p", "s")}
        self.last = {}
        self.sems = {}

    def add(self, eng, fn, after, sem=None):
        tok = Tok(sem or eng, 16 if sem else 1)
        waits = []

        def flat(x):
            if x is None:
                return
            if isinstance(x, Tok):
                x.need = True
                waits.append(x)
            else:
                for y in x:
                    flat(y)
        flat(after)
        if eng in "vap" and not sem:
            if eng in self.last:
                flat(self.last[eng])
            self.last[eng] = tok
        self.ops[eng].append((waits, fn, tok))
        return tok

    def pe(self, fn, *after):
        return self.add("t", fn, after)

    def dve(self, fn, *after):
        return self.add("v", fn, after)

    def act(self, fn, *after):
        return self.add("a", fn, after)

    def pool(self, fn, *after):
        return self.add("p", fn, after)

    def dma(self, out, in_, sem, *after):
        return self.add("s", lambda e: e.dma_start(out, in_), after, sem)

    def number(self):
        count = {}
        for eng in self.ops:
            for _, _, tok in self.ops[eng]:
                if tok.need or tok.inc == 16:
                    count[tok.sem] = count.get(tok.sem, 0) + tok.inc
                    tok.val = count[tok.sem]
        return count

    def play(self, eng, e, sem, totals):
        seen = {}
        for waits, fn, tok in self.ops[eng]:
            top = {}
            for w in waits:
                top[w.sem] = max(top.get(w.sem, 0), w.val)
            for s, v in top.items():
                if seen.get(s, 0) < v:
                    e.wait_ge(sem[s], v)
                    seen[s] = v
            ins = fn(e)
            if tok.val is not None:
                ins.then_inc(sem[tok.sem], tok.inc)
        if eng == "s":
            for s, v in totals.items():
                if s not in ("t", "v", "a", "p"):
                    e.wait_ge(sem[s], v)


class Ring:

    def __init__(self, aps):
        self.q = deque((x, ()) for x in aps)

    def take(self):
        return self.q.popleft()

    def give(self, ap, *toks):
        self.q.append((ap, toks))


def program(nc, W, WSM, LORA, PARd, CSTd, MSKd, CTX, XIN, XS, OUT, upto=99):
    Q = Queues()
    pe, dve, act, pool = Q.pe, Q.dve, Q.act, Q.pool
    ctx = ExitStack()
    with ctx:
        def sb(name, n, dt=F32):
            return ctx.enter_context(nc.sbuf_tensor(name, [128, n], dt))

        par = sb("par", PARN)
        cst = sb("cst", CSTN)
        msk = sb("msk", MSKN // 4, mybir.dt.uint32)
        msk8 = msk[:, :].bitcast(U8)
        nhalf = sb("nhalf", 1)
        smalls = sb("smalls", 48)
        xT_ = sb("xT", 16 * 256)
        wring = sb("wring", NSLOT * 2048)
        ARENA = 35200
        arena = sb("arena", ARENA)
        banks = [ctx.enter_context(nc.psum_tensor(f"bank{i}", [128, 512], F32)) for i in range(8)]

        xT = xT_[:, :].rearrange("p (k t) -> p k t", k=16)

        def P(name, i=0, w=None):
            o, n = PAR[name]
            return par[:, o + i:o + i + (n if w is None else w)]

        def C(name, i=0, w=None):
            o, n = CST[name]
            return cst[:, o + i:o + i + (n if w is None else w)]

        def M(name, i=0, w=None):
            o, n = MSK[name]
            return msk8[:, o + i:o + i + (n if w is None else w)]

        ident = C("ident")
        ones = C("ones")
        bones = C("bones")

        def bc(ap, n):
            return ap[:, None, :].broadcast_to([ap.shape[0], n, ap.shape[1]])

        def bcl(ap, n):
            return ap[:, :, None].broadcast_to([ap.shape[0], ap.shape[1], n])

        at = [0]

        def alloc(n, **dims):
            a = arena[:, at[0]:at[0] + n]
            at[0] += n
            assert at[0] <= ARENA, at[0]
            return a

        def barrier():
            return [Q.last.get("v"), Q.last.get("a"), Q.last.get("p"), Q.ops["t"][-1][2] if Q.ops["t"] else None]

        PJ = Ring([banks[i][:, :] for i in range(2)])
        PM = Ring([banks[i][:, :] for i in range(2, 8)])

        def mm(out, lhsT, rhs, start, stop, *after):
            return pe(lambda e: e.matmul(out, lhsT, rhs, start=start, stop=stop), *after)

        def tr(out, in_, *after):
            return pe(lambda e: e.transpose(out, in_, ident), *after)

        def tt(out, a, b, op, *after):
            return dve(lambda e: e.tensor_tensor(out, a, b, op), *after)

        def ts(out, a, s1, s2, op0, op1, *after):
            if s2 is None:
                return dve(lambda e: e.tensor_scalar(out, a, s1, None, op0), *after)
            return dve(lambda e: e.tensor_scalar(out, a, s1, s2, op0, op1), *after)

        def stt(out, a, s, b, op0, op1, *after):
            return dve(lambda e: e.scalar_tensor_tensor(out, a, s, b, op0, op1), *after)

        def af(out, a, func, *after, scale=1.0, bias=0.0):
            return act(lambda e: e.activation(out, a, func, scale=scale, bias=bias), *after)

        def acp(out, a, *after, scale=1.0):
            return act(lambda e: e.activation(out, a, ACT.Copy, scale=scale), *after)

        def ptt(out, a, b, op, *after):
            return pool(lambda e: e.tensor_tensor(out, a, b, op), *after)

        def cpred(out, mask, data, *after):
            return dve(lambda e: e.copy_predicated(out, mask, data), *after)

        mult, add, sub = ALU.mult, ALU.add, ALU.subtract

        l0 = [Q.dma(cst[:, :], CSTd, "ld0"), Q.dma(par[:, :], PARd, "ld1"), Q.dma(msk[:, :], MSKd, "ld2"),
              Q.dma(xT_[:, :], XIN, "ld3")]
        tx = l0[3]
        tnh = dve(lambda e: e.memset(nhalf[:, :], -0.5), l0)

        wfree = [()] * NSLOT
        wn = [0]

        def wtake():
            i = wn[0]
            wn[0] += 1
            s = i % NSLOT
            ap = wring[:, s * 2048:(s + 1) * 2048]
            t = Q.dma(ap, W[i], f"w{s}", wfree[s])
            wfree[s] = None
            return ap.rearrange("p (k n) -> p k n", k=16), t, s

        def wgive(s, *toks):
            wfree[s] = toks

        smr = Ring([smalls[:, 8 * i:8 * i + 8] for i in range(6)])

        def root(sums, n, heads, c1, c2, t, release):
            sm, fs = smr.take()
            s_ = sm[:, 0:n]
            t = ts(s_, sums, c1, c2, mult, add, t, fs)
            release(t)
            t = pool(lambda e: e.tensor_tensor(s_, s_, nhalf[:, 0:1].broadcast_to([128, n]), ALU.pow), t, tnh)
            p2, fr2 = PM.take()
            for m in range(n // heads):
                w = 128 // heads
                for e_ in range(heads):
                    l_ = sm[:, heads * m + e_:heads * m + e_ + 1].broadcast_to([128, w])
                    t2 = mm(p2[w * e_:w * e_ + w, 128 * m:128 * m + 128], l_, ident, True, True, t, fr2)
            smr.give(sm, t2)
            return p2, t2

        def rsq(sq, heads, c1, c2, *after):
            n = sq.shape[1] // 128
            ps, fr = PM.take()
            rhs = bones[:, 0:128:64] if heads == 2 else ones[:, 0:1]
            for m in range(n):
                t = mm(ps[:, heads * m:heads * m + heads], sq[:, 128 * m:128 * m + 128], rhs, True, True, fr, *after)
            return root(ps[:, 0:n * heads], n * heads, heads, c1, c2, t, lambda t: PM.give(ps, t)) + (t,)

        def norm_scale(xs, rb, sq, *txs):
            ps, fr = PM.take()
            pq, fq = PM.take()
            for g in range(4):
                ta = af(sq[:, g % 2], xs[:, 4 * g:4 * g + 4, :], ACT.Square, txs, sqf[g % 2])
                for k in range(4):
                    mm(ps[:, 0:1], sq[:, g % 2, k, 0:128], ones[:, 0:1], g == 0 and k == 0, g == 3 and k == 3, ta, fr, fq)
                    t = mm(pq[:, 0:1], sq[:, g % 2, k, 128:256], ones[:, 0:1], g == 0 and k == 0, g == 3 and k == 3)
                sqf[g % 2] = t
            s2, f2 = smr.take()
            t = acp(s2[:, 0:1], ps[:, 0:1], t, f2)
            PM.give(ps, t)
            t = acp(s2[:, 1:2], pq[:, 0:1], t)
            PM.give(pq, t)
            p2, t2 = root(s2[:, 0:2], 2, 1, 1.0 / 2048, EPS, t, lambda t: smr.give(s2, t))
            t2 = acp(rb, p2[:, 0:256], t2)
            PM.give(p2, t2)
            return t2

        sqf = [None, None]

        def project(ntok0, ntok1, hT, th, evac, width=128):
            w, tw, s = wtake()
            ps, fr = PJ.take()
            for k in range(16):
                t = mm(ps[:, 0:ntok1 - ntok0], w[:, k, :], hT[:, k, ntok0:ntok1], k == 0, k == 15, tw, fr, th)
                if k % 4 == 3 and k < 15:
                    yield
            wgive(s, t)
            PJ.give(ps, *evac(ps[:, 0:ntok1 - ntok0], t))
            yield

        def run(*gens):
            gens = list(gens)
            while gens:
                alive = []
                for g in gens:
                    try:
                        next(g)
                        alive.append(g)
                    except StopIteration:
                        pass
                gens = alive

        def layer(l, tx):
            at[0] = 0
            bar = barrier()
            SC = 128 ** -0.5
            LI = 0.8 - 0.6 * math.exp(-0.3 * l)
            hT_ = alloc(4096)
            mix_ = alloc(4096)
            hT = hT_.rearrange("p (k t) -> p k t", k=16)
            mix = mix_.rearrange("p (k t) -> p k t", k=16)
            rb = alloc(256)
            wsm_ = alloc(320)
            wsm = wsm_.rearrange("p (k n) -> p k n", k=16)
            sq = mix_[:, 0:2048].rearrange("p (g k t) -> p g k t", g=2, k=4)
            tws = Q.dma(wsm_, WSM[l], f"sm{l}", bar)
            tr_ = norm_scale(xT, rb, sq, tx, bar)
            th = [None] * 1
            for k in range(16):
                t = stt(hT[:, k, :], xT[:, k, :], P("ng", l * 16 + k, 1), rb, mult, mult, tr_, bar)
            th = t

            fl = alloc(48).rearrange("p (a b) -> p a b", b=8)
            ft = fl[:, 0:1, :].rearrange("p a b -> p (a b)")
            aT = alloc(256)
            ps, fr = PM.take()
            for m in range(2):
                for k in range(16):
                    t = mm(ps[:, 4 * m:4 * m + 4], hT[:, k, 128 * m:128 * m + 128], wsm[:, k, 0:4], k == 0, k == 15, th, tws, fr)
            for k in range(16):
                t = mm(ps[0:16, 256:512], wsm[:, k, 4:20], hT[:, k, :], k == 0, k == 15)
            t1 = tt(ft.rearrange("p (m h) -> p m h", m=2), ps[:, 0:8].rearrange("p (m h) -> p m h", m=2),
                    bc(P("fb", 4 * l, 4), 2), add, t)
            t2 = acp(aT[0:16, :], ps[0:16, 256:512], t, t1)
            PM.give(ps, t1, t2)

            def logsig(z, tmp, tz):
                t = af(tmp, z, ACT.Abs, tz)
                t = af(tmp, tmp, ACT.Exp, t, scale=-1.0)
                t = af(tmp, tmp, ACT.Ln, t, bias=1.0)
                return stt(z, z, 0.0, tmp, ALU.min, sub, t)
            tf = logsig(ft, fl[:, 1, :], t1)

            lam = fl[:, 2, :]
            lp = fl[:, 3, :]
            lamp = P("lam", 4 * l, 4)
            t = tt(lp[0:64, 0:2], lamp[0:64, 0:4:2], lamp[0:64, 1:4:2], mult)
            ps, fr = PM.take()
            t = mm(ps[:, 0:2], ones[0:64, :], lp[0:64, 0:2], True, True, t, fr)
            t = af(lam[:, 0:2], ps[:, 0:2], ACT.Exp, t)
            PM.give(ps, t)
            t = tt(lam[:, 2:3], lam[:, 1:2], lam[:, 0:1], sub, t)
            tlam = ts(lam[:, 3:4], lam[:, 2:3], LI, None, sub, None, t)

            qk = [[alloc(1024).rearrange("p (h t) -> p h t", h=4) for _ in range(2)] for _ in range(2)]
            vt = [alloc(1024).rearrange("p (m c) -> p m c", m=2) for _ in range(2)]
            gt = [alloc(1024).rearrange("p (h t) -> p h t", h=4) for _ in range(2)]
            raw = Ring([alloc(256) for _ in range(3)])
            LR = Ring([alloc(384) for _ in range(4)])
            PT = Ring([alloc(384) for _ in range(2)])
            OR = Ring([alloc(256) for _ in range(4)])
            SM = Ring([alloc(8) for _ in range(4)])
            T = {}

            def ev_copy(key, dst, scale=1.0, free=None):
                def f(ps, t):
                    T[key] = acp(dst, ps, t, free() if free else None, scale=scale)
                    return [T[key]]
                return f

            def ev_rope(key, dst, scale, nm, free):
                def f(ps, t):
                    r, fr = raw.take()
                    t0 = acp(r, ps, t, fr, scale=scale)
                    p2, fr2 = PM.take()
                    t1 = mm(p2[:, 0:256], C("permd" if nm == "d" else "permm"), r, True, True, t0, fr2)
                    o, fo = OR.take()
                    t2 = tt(o, p2[:, 0:256], C("S" + nm), mult, t1, fo)
                    PM.give(p2, t2)
                    t3 = ptt(r, r, C("C" + nm), mult, t0, t1, tnh)
                    T[key] = tt(dst, o, r, add, t3, t2, free())
                    raw.give(r, T[key])
                    OR.give(o, T[key])
                    return [t0]
                return f

            def ev_v(key, dst, free):
                def f(ps, t):
                    r, fr = raw.take()
                    t0 = acp(r, ps, t, fr)
                    p2, fr2 = PM.take()
                    t1 = tr(p2[:, 0:128], r[:, 0:128], t0, fr2)
                    t1 = tr(p2[:, 128:256], r[:, 128:256])
                    raw.give(r, t1)
                    T[key] = acp(dst, p2[:, 0:256].rearrange("p (m c) -> p m c", m=2), t1, free())
                    PM.give(p2, T[key])
                    return [t0]
                return f

            def ev_gate(key, dst, free):
                def f(ps, t):
                    t0 = af(dst, ps, ACT.Tanh, t, free(), scale=0.5)
                    T[key] = stt(dst, dst, 1.0, ps, add, mult, t0)
                    return [T[key]]
                return f

            groups = ["fox", "diff", "moba", "gla"]

            def projections():
                for gi, g in enumerate(groups):
                    b = gi % 2
                    while gi >= 2 and (groups[gi - 2], "done") not in T:
                        yield

                    def free(gi=gi):
                        return T[(groups[gi - 2], "done")] if gi >= 2 else bar
                    if g in ("fox", "diff", "moba"):
                        scs = {"fox": SC, "diff": 64 ** -0.5, "moba": SC}[g]
                        for j in range(2):
                            for h in range(4):
                                key = (g, "qk"[j], h)
                                dst = qk[b][j][:, h, :]
                                s = scs if j == 0 else 1.0
                                if g == "fox":
                                    yield from project(0, 256, hT, th, ev_copy(key, dst, s, free))
                                else:
                                    yield from project(0, 256, hT, th, ev_rope(key, dst, s, g[0], free))
                    else:
                        for j in range(2):
                            for h in range(2):
                                yield from project(0, 256, hT, th, ev_copy((g, "qk"[j], h), qk[b][j][:, h, :],
                                                                           0.125 if j == 0 else 1.0, free))
                    for h in range(4):
                        yield from project(0, 256, hT, th, ev_v((g, "v", h), vt[b][:, :, 128 * h:128 * h + 128], free))
                    for h in range(4):
                        yield from project(0, 256, hT, th, ev_gate((g, "g", h), gt[b][:, h, :], free))

            def wait(*keys):
                while not all(k in T for k in keys):
                    yield

            def softmax(ps, tps, nrm=True):
                L, fL = LR.take()
                sm, fs = SM.take()
                t = tt(L, ps[:, 0:384], C("mask3"), add, tps, fL)
                PM.give(ps, t)
                t = dve(lambda e: e.tensor_reduce(sm[:, 0:1], L[:, 0:128], AX.X, ALU.max, negate=True), t, fs)
                t = dve(lambda e: e.tensor_reduce(sm[:, 1:2], L[:, 128:384], AX.X, ALU.max, negate=True))
                t1 = act(lambda e: e.activation(L[:, 0:128], L[:, 0:128], ACT.Exp, bias=sm[:, 0:1], scale=1.0, accum_out=sm[:, 2:3]), t)
                t2 = act(lambda e: e.activation(L[:, 128:384], L[:, 128:384], ACT.Exp, bias=sm[:, 1:2], scale=1.0, accum_out=sm[:, 3:4]), t1)
                t3 = dve(lambda e: e.reciprocal(sm[:, 4:6], sm[:, 2:4]), t2)
                return L, sm, t3

            def finish_rms(o, to, gname, gidx):
                s, fs = OR.take()
                t = af(s, o, ACT.Square, to, fs)
                p2, t, tm = rsq(s, 1, 1.0 / 128, EPS, t)
                OR.give(s, tm)
                t = stt(o, o, P(gname, gidx, 1), p2[:, 0:256], mult, mult, t)
                PM.give(p2, t)
                return t

            def pv(g, gi, h, PTt, tpt, b):
                ps, fr = PM.take()
                V = vt[b]
                mm(ps[:, 0:128], V[:, 0, 128 * h:128 * h + 128], PTt[:, 0:128], True, True, tpt, fr, T[(g, "v", h)])
                mm(ps[:, 128:256], V[:, 0, 128 * h:128 * h + 128], PTt[:, 128:256], True, False)
                t = mm(ps[:, 128:256], V[:, 1, 128 * h:128 * h + 128], PTt[:, 256:384], False, True)
                return ps, t

            def attend():
                for gi, g in enumerate(groups[:3]):
                    b = gi % 2
                    q, kk_ = qk[b]
                    last = []
                    for h in range(4):
                        yield from wait((g, "q", h), (g, "k", h))
                        res = []
                        for sub_ in range(2 if g == "diff" else 1):
                            pr = slice(64 * sub_, 64 * sub_ + 64) if g == "diff" else slice(0, 128)
                            extra = g == "fox"
                            if extra:
                                f1, ff = LR.take()
                                ta = ts(f1[:, 0:128], C("GT"), ft[:, h:h + 1], None, mult, None, tf, ff)
                                ta = ts(f1[:, 128:384], C("G1"), ft[:, 4 + h:5 + h], None, mult, None, tf)
                            ps, fr = PM.take()
                            t = mm(ps[:, 0:128], q[pr, h, 0:128], kk_[pr, h, 0:128], True, not extra, T[(g, "q", h)], T[(g, "k", h)], fr)
                            if extra:
                                t = mm(ps[:, 0:128], C("LE"), f1[:, 0:128], False, True, ta)
                            t = mm(ps[:, 128:384], q[pr, h, 128:256], kk_[pr, h, 0:256], True, not extra)
                            if extra:
                                mm(ps[:, 128:256], ones, f1[:, 0:128], False, False)
                                t = mm(ps[:, 128:384], C("LE"), f1[:, 128:384], False, True)
                                LR.give(f1, t)
                            yield
                            res.append(softmax(ps, t))
                        yield
                        L, sm, t3 = res[0]
                        t = ts(L[:, 0:128], L[:, 0:128], sm[:, 4:5], None, mult, None, t3)
                        t = ts(L[:, 128:384], L[:, 128:384], sm[:, 5:6], None, mult, None, t3)
                        if g == "diff":
                            L2, sm2, t4 = res[1]
                            t = ts(sm2[:, 4:6], sm2[:, 4:6], lam[:, 3:4], None, mult, None, t4, tlam)
                            t = stt(L[:, 0:128], L2[:, 0:128], sm2[:, 4:5], L[:, 0:128], mult, add, t)
                            t = stt(L[:, 128:384], L2[:, 128:384], sm2[:, 5:6], L[:, 128:384], mult, add, t)
                            LR.give(L2, t)
                            SM.give(sm2, t)
                        SM.give(sm, t)
                        ps, fr = PM.take()
                        for j in range(3):
                            t2 = tr(ps[:, 128 * j:128 * j + 128], L[:, 128 * j:128 * j + 128], t, fr)
                        LR.give(L, t2)
                        p_, fp = PT.take()
                        t2 = acp(p_, ps[:, 0:384], t2, fp)
                        PM.give(ps, t2)
                        yield from wait((g, "v", h), (g, "g", h))
                        ps, t = pv(g, gi, h, p_, t2, b)
                        PT.give(p_, t)
                        m = mix[:, 4 * gi + h, :]
                        if g == "diff":
                            o, fo = OR.take()
                            t = acp(o, ps[:, 0:256], t, fo)
                            PM.give(ps, t)
                            yield
                            t = finish_rms(o, t, "dng", l)
                            t = stt(m, o, 0.5 * (1.0 - LI), gt[b][:, h, :], mult, mult, t, T[(g, "g", h)])
                            OR.give(o, t)
                        else:
                            t = stt(m, ps[:, 0:256], 0.5, gt[b][:, h, :], mult, mult, t, T[(g, "g", h)])
                            PM.give(ps, t)
                        T[("mix", 4 * gi + h)] = t
                        last += [t, t2]
                        yield
                    T[(g, "done")] = last + barrier()

            la = alloc(512).rearrange("p (m t) -> p m t", m=2)
            cum = alloc(512).rearrange("p (m t) -> p m t", m=2)
            ee = alloc(512).rearrange("p (m t) -> p m t", m=2)
            qe = alloc(512).rearrange("p (m t) -> p m t", m=2)
            ke = alloc(512).rearrange("p (m t) -> p m t", m=2)
            ST = alloc(1024).rearrange("p (u t) -> p u t", u=8)
            S01 = alloc(512).rearrange("p (u t) -> p u t", u=4)

            def gla():
                b = 1
                q, kk_ = qk[b]
                tz = dve(lambda e: e.memset(ST, 0.0), bar)
                ps, fr = PM.take()
                for m in range(2):
                    t = mm(ps[:, 256 * m:256 * m + 256], P("wa2", 256 * l + 128 * m, 128)[0:16, :], aT[0:16, :], True, True, t2a, fr)
                for m in range(2):
                    t = ts(la[:, m, :], ps[:, 256 * m:256 * m + 256], P("gba", 2 * l + m, 1), None, add, None, t)
                PM.give(ps, t)
                t = logsig(la, ee, t)
                t = ts(la, la, 1.0 / 16, None, mult, None, t)
                for m in range(2):
                    t = dve(lambda e, m=m: e.tensor_tensor_scan(cum[:, m, :], C("ones", 0, 1).broadcast_to([128, 256]), la[:, m, :],
                                                                0.0, mult, add), t)
                tcum = t
                yield
                yield from wait(*[("gla", j, h) for j in "qk" for h in range(2)])
                tq = [T[("gla", j, h)] for j in "qk" for h in range(2)]
                free_e = free_qk = None
                for lv in list(range(7, -2, -1)):
                    if lv >= 0:
                        w = 1 << lv
                        cv = cum.rearrange("p m (n two w) -> p (m n) two w", two=2, w=w)
                        ev = ee.rearrange("p m (n two w) -> p (m n) two w", two=2, w=w)
                        n = 512 // (2 * w)
                        ref = cv[:, :, 0, w - 1:w].broadcast_to([128, n, w])
                        t = tt(ev[:, :, 0, :], ref, cv[:, :, 0, :], sub, tcum, free_e)
                        t = tt(ev[:, :, 1, :], cv[:, :, 1, :], ref, sub)
                        t = af(ee, ee, ACT.Exp, t)
                        tq1 = tt(qe, q[:, 0:2, :], ee, mult, t, tq, free_qk)
                        tk1 = ptt(ke, kk_[:, 0:2, :], ee, mult, t, tq, free_qk)
                        free_e = [tq1, tk1]
                        qa, ka, td = qe, ke, [tq1, tk1]
                    else:
                        qa, ka, td = q[:, 0:2, :], kk_[:, 0:2, :], tq
                    pe_ = [PM.take() for _ in range(2)]
                    for j in range(4 if lv < 7 else 2):
                        m, hh = (j // 2, j % 2) if lv < 7 else (0, j)
                        ks = slice(128 * m, 128 * m + 128)
                        qsl = ks if lv < 7 else slice(128, 256)
                        for e_ in range(2):
                            pr = slice(64 * e_, 64 * e_ + 64)
                            t = mm(pe_[e_][0][:, 128 * j:128 * j + 128], ka[pr, hh, ks], qa[pr, hh, qsl], True, True, td, pe_[e_][1])
                    free_qk = t
                    for e_ in range(2):
                        ps = pe_[e_][0]
                        if lv == 7:
                            t1 = acp(S01[:, 2 * e_:2 * e_ + 2, :], ps[:, 0:256].rearrange("p (u t) -> p u t", u=2), t)
                            ts01 = t1
                        else:
                            mk = M("gla", 128 * (lv if lv >= 0 else 7), 128)
                            t1 = cpred(ST[:, 4 * e_:4 * e_ + 4, :], bc(mk, 4), ps.rearrange("p (u t) -> p u t", u=4), t, tz)
                            tst = t1
                        PM.give(ps, t1)
                    yield
                for h in range(4):
                    yield from wait(("gla", "v", h), ("gla", "g", h))
                    ps, fr = PM.take()
                    V = vt[b]
                    hs = slice(128 * h, 128 * h + 128)
                    e_, hh = h % 2, h // 2
                    mm(ps[:, 0:128], V[:, 0, hs], ST[:, 4 * e_ + hh, :], True, True, tst, ts01, fr, T[("gla", "v", h)])
                    mm(ps[:, 128:256], V[:, 0, hs], S01[:, 2 * e_ + hh, :], True, False)
                    t = mm(ps[:, 128:256], V[:, 1, hs], ST[:, 4 * e_ + 2 + hh, :], False, True)
                    o, fo = OR.take()
                    t = acp(o, ps[:, 0:256], t, fo)
                    PM.give(ps, t)
                    t = finish_rms(o, t, "gng", l)
                    t = stt(mix[:, 12 + h, :], o, 0.5, gt[b][:, h, :], mult, mult, t, T[("gla", "g", h)])
                    OR.give(o, t)
                    T[("mix", 12 + h)] = t
                    yield
            t2a = t2
            run(projections(), attend(), gla())
            tm = [T[("mix", i)] for i in range(16)]
            txl = []

            def ev_res(c):
                def f(ps, t):
                    t = tt(xT[:, c, :], xT[:, c, :], ps, add, t)
                    txl.append(t)
                    return [t]
                return f
            run((x for c in range(16) for x in project(0, 256, mix, tm, ev_res(c))))
            return txl

        def store(tx):
            Q.dma(OUT, xT_[:, :], "out", tx)

        def final_norm(tx, pname):
            at[0] = 0
            bar = barrier()
            rb = alloc(256)
            sq = alloc(2048).rearrange("p (g k t) -> p g k t", g=2, k=4)
            t = norm_scale(xT, rb, sq, tx, bar)
            for k in range(16):
                t = stt(xT[:, k, :], xT[:, k, :], P(pname, k, 1), rb, mult, mult, t)
            return t

        def second(tx):
            at[0] = 0
            bar = barrier()
            mod = alloc(192).rearrange("p (n two) -> p n two", two=2)
            sc_ = alloc(64)
            scv = sc_[:, 0:32].rearrange("p (k two) -> p k two", two=2)
            A_ = alloc(48).rearrange("p (j k) -> p j k", j=3)
            hT = alloc(8192).rearrange("p (k t) -> p k t", k=16)
            ya = alloc(2048).rearrange("p (k t) -> p k t", k=8)
            rb = alloc(512)
            mark = at[0]
            cT = alloc(4096).rearrange("p (k t) -> p k t", k=16)
            sq = alloc(4096).rearrange("p (g k t) -> p g k t", g=2, k=4)
            tctx = Q.dma(cT, CTX.rearrange("p (k t) -> p k t", k=16), "ctx", bar)
            t = af(sc_[:, 32:64], P("c"), ACT.Tanh, bar, scale=0.5)
            t = stt(sc_[:, 0:32], sc_[:, 32:64], 1.0, P("c"), add, mult, t)
            tsc = ts(sc_[:, 0:32], sc_[:, 0:32], 0.5, None, mult, None, t)
            psm, fr = PM.take()
            for n in range(NMOD):
                w, tw, s = wtake()
                for k in range(16):
                    t = mm(psm[:, 2 * n:2 * n + 2], w[:, k, :], scv[:, k, :], k == 0, k == 15, tw, fr, tsc)
                wgive(s, t)
            t = tt(mod, psm[:, 0:192].rearrange("p (n two) -> p n two", two=2), bcl(P("modb"), 2), add, t)
            PM.give(psm, t)
            for j, (pn, sc0, col) in enumerate((("n1", 16, 0), ("n1", 16, 1), ("n2", 64, 0))):
                t = stt(A_[:, j, :], mod[:, sc0:sc0 + 16, col], 1.0, P(pn), add, mult, t)
            tmod = t
            sqc = sq
            sq1 = sq.rearrange("p g k t -> p (g k t)")[:, 0:2048].rearrange("p (g k t) -> p g k t", g=2, k=4)
            t = norm_scale(xT, rb[:, 0:256], sq1, tx, bar)
            t2 = norm_scale(cT, rb[:, 256:512], sq1, tctx)
            for k in range(16):
                t = stt(hT[:, k, 0:256], xT[:, k, :], A_[:, 0, k:k + 1], rb[:, 0:256], mult, mult, t, tmod, t2)
                ta = af(hT[:, k, 0:256], hT[:, k, 0:256], ACT.Identity, t, bias=mod[:, k, 0:1])
                t = stt(hT[:, k, 256:512], cT[:, k, :], A_[:, 1, k:k + 1], rb[:, 256:512], mult, mult, t2)
                ta = af(hT[:, k, 256:512], hT[:, k, 256:512], ACT.Identity, t, bias=mod[:, k, 1:2])
            th = ta
            at[0] = mark
            bar = barrier()
            tspill = Q.dma(XS, xT_[:, :], "spill", bar)
            bar = bar + [tspill]

            mu4 = alloc(168).rearrange("p (n y) -> p n y", y=6)
            mu1 = alloc(28)
            T = {}
            tmu = tt(mu4, bcl(P("mu"), 6), bc(C("type"), 28), mult, bar)
            tmu = ts(mu1, P("mu"), -1.0, 1.0, mult, add, bar)
            tw_ = alloc(512)
            xa = alloc(512)
            sg = alloc(512).rearrange("p (m t) -> p m t", m=2)
            ab = alloc(128).rearrange("p (q n) -> p q n", q=4)
            half_mark = at[0]
            zr = Ring([alloc(512) for _ in range(2)])

            def mixshift(dst, ps, t, n, rows, ctx_too, free):
                z, fz = zr.take()
                N = 512 if ctx_too else 256
                t0 = acp(z[0:rows, 0:N], ps[0:rows, 0:N], t, fz)
                t1 = ts(dst[0:rows, 0:N], z[0:rows, 0:N], mu1[0:rows, n:n + 1], None, mult, None, t0, free, tmu)
                x4 = z[0:rows, 0:256].rearrange("p (r c) -> p r c", r=4)
                d4 = dst[0:rows, 0:256].rearrange("p (r c) -> p r c", r=4)

                def acc(o, i, y):
                    return stt(o, i, mu4[0:rows, n, y:y + 1], o, mult, add)
                acc(d4[:, :, 1:64], x4[:, :, 0:63], 0)
                acc(d4[:, :, 0:63], x4[:, :, 1:64], 1)
                acc(dst[0:rows, 64:256], z[0:rows, 0:192], 2)
                t1 = acc(dst[0:rows, 0:192], z[0:rows, 64:256], 3)
                if ctx_too:
                    acc(dst[0:rows, 257:512], z[0:rows, 256:511], 4)
                    t1 = acc(dst[0:rows, 256:511], z[0:rows, 257:512], 5)
                zr.give(z, t1)
                return t1, t0

            def ev_w(ps, t):
                t1, t0 = mixshift(tw_, ps, t, 24, 96, True, bar)
                T["tw"] = af(tw_[0:96, :], tw_[0:96, :], ACT.Tanh, t1)
                r, fz = zr.take()
                t2 = acp(r[96:128, :], ps[96:128, :], t, fz)
                p2, fr = PM.take()
                for q_ in range(4):
                    t3 = mm(p2[:, 32 * q_:32 * q_ + 32], r[96:128, 128 * q_:128 * q_ + 128], ident[96:128, 96:128], True, True, t2, fr)
                zr.give(r, t3)
                T["ab"] = acp(ab, p2[:, 0:128].rearrange("p (q n) -> p q n", q=4), t3)
                PM.give(p2, T["ab"])
                return [t0, t2]

            def ev_a(ps, t):
                t1, t0 = mixshift(xa, ps, t, 25, 128, True, bar)
                T["xa"] = t1
                return [t0]

            def ev_g(m):
                def f(ps, t):
                    t1, t0 = mixshift(sg[:, m, :], ps, t, 26 + m, 128, False, bar)
                    t1 = af(sg[:, m, :], sg[:, m, :], ACT.Tanh, t1, scale=0.5)
                    T[("sg", m)] = ts(sg[:, m, :], sg[:, m, :], 0.5, 0.5, mult, add, t1)
                    return [t0]
                return f
            run((x for g in (project(0, 512, hT, th, ev_w), project(0, 512, hT, th, ev_a), project(0, 256, hT, th, ev_g(0)),
                             project(0, 256, hT, th, ev_g(1))) for x in g))

            def cols(ap, w, par_):
                return ap.rearrange("p (n two w) -> p n two w", two=2, w=w)[:, :, par_, :]

            def inverse(d, NA, tna, X, XT, Qs, qfree, frX, U=8):
                par_ = d
                t_x = pool(lambda e: e.tensor_copy(X.rearrange("p (u s) -> p u s", u=U), bc(ident, U)), frX, bar)
                t_xt = pool(lambda e: e.tensor_copy(XT.rearrange("p (u s) -> p u s", u=U), bc(ident, U)), frX, bar)
                tX = tXT = None
                for lv in range(7):
                    w = 1 << lv
                    mk = M("lev", (d * 7 + lv) * 64, 64)
                    ps, fr = PM.take()
                    for u in range(U):
                        sl = slice(128 * u, 128 * u + 128)
                        r = cols(ident, w, par_) if lv == 0 else cols(X[:, sl], w, par_)
                        t = mm(ps[:, 64 * u:64 * u + 64].rearrange("p (n w) -> p n w", w=w), NA[:, sl], r, True, True, tna, fr, tX, t_x)

                    def mview():
                        return mk.rearrange("p (n w) -> p n w", w=w)[:, None, :, :].broadcast_to([128, U, 64 // w, w])

                    def dview(buf):
                        return buf.rearrange("p (u n two w) -> p u n two w", u=U, two=2, w=w)[:, :, :, par_, :]
                    p4 = ps[:, 0:64 * U].rearrange("p (u n w) -> p u n w", u=U, w=w)
                    yield
                    if lv == 0:
                        tX = cpred(dview(X), mview(), p4, t, t_x)
                        PM.give(ps, tX)
                        m0 = M("xt0", d * 64, 64)[:, None, :].broadcast_to([128, U, 64])
                        xv = XT.rearrange("p (u n two) -> p u n two", u=U, two=2)[:, :, :, 1 - par_]
                        nv = NA.rearrange("p (u n two) -> p u n two", u=U, two=2)[:, :, :, 1 - par_]
                        tXT = cpred(xv, m0, nv, tna, t_xt)
                        continue
                    qb = Qs[lv % 2]
                    tq = cpred(dview(qb), mview(), p4, t, qfree[lv % 2])
                    PM.give(ps, tq)
                    if lv < 6:
                        ps, fr = PM.take()
                        for u in range(U):
                            sl = slice(128 * u, 128 * u + 128)
                            t1 = mm(ps[:, 64 * u:64 * u + 64].rearrange("p (n w) -> p n w", w=w), XT[:, sl], cols(qb[:, sl], w, par_), True, True, tq, tXT, fr)
                    ps2, fr2 = PM.take()
                    for u in range(U):
                        sl = slice(128 * u, 128 * u + 128)
                        t2 = mm(ps2[:, 64 * u:64 * u + 64].rearrange("p (n w) -> p n w", w=w), qb[:, sl], cols(XT[:, sl], w, 1 - par_), True, True, tq, tXT, fr2)
                    yield
                    if lv < 6:
                        tX = acp(cols(X, w, par_), ps[:, 0:64 * U].rearrange("p (n w) -> p n w", w=w), t1, t)
                        PM.give(ps, tX)
                    o2, i2 = cols(XT, w, 1 - par_), ps2[:, 0:64 * U].rearrange("p (n w) -> p n w", w=w)
                    if lv % 2:
                        tXT = acp(o2, i2, t2)
                    else:
                        tXT = dve(lambda e, o2=o2, i2=i2: e.tensor_copy(o2, i2), t2)
                    PM.give(ps2, tXT)
                    idv = ident.rearrange("p (n two w) -> p n two w", two=2, w=w)[:, :, par_, :][:, None, :, :].broadcast_to([128, U, 64 // w, w])
                    dq = dview(qb)
                    qfree[lv % 2] = pool(lambda e, dq=dq, idv=idv: e.tensor_copy(dq, idv), t2)
                    yield
                return tXT

            mark2 = at[0]
            xat = [0]

            def xbuf(n):
                a = xT_[:, xat[0]:xat[0] + n]
                xat[0] += n
                return a
            kT = xbuf(512)
            vT = xbuf(512)
            rT = alloc(256)
            kkn = alloc(512)
            rrk = alloc(256)
            Vt = alloc(512).rearrange("p (q c) -> p q c", q=4)
            lo = alloc(768).rearrange("p (j c) -> p j c", j=6)
            tmp = [xbuf(512) for _ in range(5)]
            D = []
            for d in range(2):
                kb_ = alloc(1024)
                D.append(dict(Kd=kb_[:, 0:512], Bd=kb_[:, 512:1024], X=kb_, KK=alloc(512), Rd=alloc(256), Kt=alloc(512), Bt=alloc(512),
                              NA=alloc(1024), AK=alloc(1024), RK=alloc(512), RB=alloc(512), XT=alloc(1024),
                              Q=[alloc(1024) for _ in range(2)], H=alloc(128), RU=[alloc(128) for _ in range(2)], es=alloc(8),
                              Y=xbuf(256), qf=[None, None]))
            ys = [tmp[j][:, 0:256] for j in range(3)]
            loq = [None, None]
            lot = {}

            def lload(c):
                lot[c] = Q.dma(lo, LORA[c].rearrange("p (j n) -> p j n", j=6), "lora", loq[0], bar)
            lload(0)
            tz = None
            for d in range(2):
                for nm in ("NA", "AK", "RK", "RB", "H"):
                    b_ = D[d][nm]
                    tz = dve(lambda e, b_=b_: e.memset(b_, 0.0), bar)
                for qb in D[d]["Q"]:
                    tq0 = pool(lambda e, qb=qb: e.tensor_copy(qb.rearrange("p (u s) -> p u s", u=8), bc(ident, 8)), bar)
                D[d]["qf"] = [tq0, tq0]
            tyl = []

            def branch_a():
                prev_done = bar
                for c in range(8):
                    E = {}

                    def ev(dst, n, key, both):
                        def f(ps, t):
                            t1, t0 = mixshift(dst, ps, t, n, 128, both, prev_done)
                            E[key] = t1
                            return [t0]
                        return f
                    yield from project(0, 256, hT, th, ev(rT, c, "r", False))
                    yield from project(0, 512, hT, th, ev(kT, 8 + c, "k", True))
                    yield from project(0, 512, hT, th, ev(vT, 16 + c, "v", True))
                    tl = lot[c]
                    L6 = lo
                    t = ts(kkn, kT, P("kk", c, 1), None, mult, None, E["k"], prev_done)
                    t = af(tmp[0], kkn, ACT.Square, t, prev_done)
                    ps, t, _ = rsq(tmp[0], 2, 1.0, 1e-12, t)
                    tkk = tt(kkn, kkn, ps, mult, t)
                    PM.give(ps, tkk)
                    trk = ts(rrk, rT, P("rk", c, 1), None, mult, None, E["r"], prev_done)
                    ps, fr = PM.take()
                    for q_ in range(4):
                        t = tr(ps[:, 128 * q_:128 * q_ + 128], vT[:, 128 * q_:128 * q_ + 128], E["v"], fr)
                    tV = acp(Vt, ps.rearrange("p (q c) -> p q c", q=4), t, prev_done)
                    PM.give(ps, tV)
                    psb, frb = PM.take()
                    yield

                    def prep(d):
                        G = D[d]
                        z, a_, cc, e1, e2 = tmp
                        ps, fr = PM.take()
                        t = mm(ps, L6[0:96, d, :], tw_[0:96, :], True, True, T["tw"], tl, fr)
                        t = af(z, ps, ACT.Tanh, t, twh, Q.last["v"], Q.last["p"], scale=0.5, bias=w0h[:, 8 * d + c:8 * d + c + 1])
                        PM.give(ps, t)
                        k0 = -0.5 * math.exp(-0.5)
                        tlw = ts(z, z, k0, k0, mult, add, t)
                        ps, fr = PM.take()
                        t = mm(ps, L6[:, 2 + d, :], xa, True, True, T["xa"], fr)
                        t = af(a_, ps, ACT.Tanh, t, scale=0.5, bias=a0h[:, 8 * d + c:8 * d + c + 1])
                        PM.give(ps, t)
                        ta = ts(a_, a_, 0.5, 0.5, mult, add, t)
                        if d == 0:
                            t = dve(lambda e: e.tensor_tensor_scan(cc, C("scan"), z, 0.0, mult, add), tlw)
                        else:
                            t = dve(lambda e: e.tensor_tensor_scan(cc[:, ::-1], C("scan"), z[:, ::-1], 0.0, mult, add), tlw)
                        c4 = cc.rearrange("p (q t) -> p q t", q=4)
                        mid = 63 + d
                        end = 127 if d == 0 else 0
                        order = (2, 3, 0, 1) if d == 0 else (3, 2, 1, 0)
                        for i, q_ in enumerate(order[:3]):
                            nq = order[i + 1]
                            t = tt(G["es"][:, q_:q_ + 1], c4[:, q_, end:end + 1], c4[:, q_, mid:mid + 1], sub, t)
                            t = tt(G["es"][:, q_:q_ + 1], G["es"][:, q_:q_ + 1], c4[:, nq, mid:mid + 1], add)
                        lastq = order[3]
                        t = ts(G["es"][:, lastq:lastq + 1], G["es"][:, order[0]:order[0] + 1], 0.0, None, mult, None)
                        G["tes"] = af(G["es"][:, 0:4], G["es"][:, 0:4], ACT.Exp, t)
                        t = ts(G["es"][:, 4:8], c4[:, :, mid], 1.0, None, mult, None)
                        t = tt(c4, c4, bcl(G["es"][:, 4:8], 128), sub, t)
                        t1 = ts(e1, a_, -1.0, P("ka", c, 1), add, mult, ta)
                        tkd = stt(e1, e1, 1.0, kT, add, mult, E["k"])
                        pr_ = G["Rd"]
                        tp_ = tt(pr_, rrk, e1[:, 0:256], mult, trk)
                        tbon = mm(psb[:, 0:256], bones, pr_, d == 0, d == 1, tp_, frb)
                        tba = tt(a_, a_, kkn, mult, tkk)
                        te = af(e2, cc, ACT.Exp, t, scale=-1.0)
                        tKd = tt(G["Kd"], e1, e2, mult, te)
                        tBd = stt(G["Bd"], a_, -1.0, e2, mult, mult)
                        te = af(e2[:, 0:256], cc[:, 0:256], ACT.Exp, tBd)
                        tRd = tt(G["Rd"], rT, e2[:, 0:256], mult, te, tbon, E["r"])
                        t = tt(cc, cc, z, sub, te)
                        te = af(e2, cc, ACT.Exp, t, tRd)
                        tKK = tt(G["KK"], kkn, e2, mult, te)
                        return tbon, [tKd, tBd, tRd, tKK]

                    def scores(d, tin):
                        G = D[d]
                        sm = M("strict", 128 * d, 128)
                        im = M("incl", 128 * d, 128)
                        for nm, src in (("Kt", "Kd"), ("Bt", "Bd")):
                            ps, fr = PM.take()
                            for q_ in range(4):
                                t = tr(ps[:, 128 * q_:128 * q_ + 128], G[src][:, 128 * q_:128 * q_ + 128], tin, fr)
                            G["t" + nm] = acp(G[nm], ps, t)
                            PM.give(ps, G["t" + nm])
                        for nm, src in (("NA", "Bd"), ("AK", "Kd")):
                            pe_ = [PM.take() for _ in range(2)]
                            for q_ in range(4):
                                sl = slice(128 * q_, 128 * q_ + 128)
                                for e_ in range(2):
                                    pr = slice(64 * e_, 64 * e_ + 64)
                                    t1 = mm(pe_[e_][0][:, sl], G[src][pr, sl], G["KK"][pr, sl], True, True, tin, pe_[e_][1])
                            for e_ in range(2):
                                ps = pe_[e_][0]
                                t = cpred(G[nm][:, 512 * e_:512 * e_ + 512].rearrange("p (u t) -> p u t", u=4), bc(sm, 4),
                                          ps.rearrange("p (u t) -> p u t", u=4), t1, tz)
                                PM.give(ps, t)
                            G["t" + nm] = t
                            yield
                        pe_ = [PM.take() for _ in range(2)]
                        for j, src in enumerate(("Bd", "Kd")):
                            for q_ in range(2):
                                sl = slice(128 * q_, 128 * q_ + 128)
                                for e_ in range(2):
                                    pr = slice(64 * e_, 64 * e_ + 64)
                                    o = 256 * j + 128 * q_
                                    t1 = mm(pe_[e_][0][:, o:o + 128], G[src][pr, sl], G["Rd"][pr, sl], True, True, tin, pe_[e_][1])
                        for e_ in range(2):
                            ps = pe_[e_][0]
                            for j, nm in enumerate(("RB", "RK")):
                                t = cpred(G[nm][:, 256 * e_:256 * e_ + 256].rearrange("p (u t) -> p u t", u=2), bc(im, 2),
                                          ps[:, 256 * j:256 * j + 256].rearrange("p (u t) -> p u t", u=2), t1, tz)
                                G["t" + nm] = t
                            PM.give(ps, t)
                        G["tsc"] = t1
                        yield

                    def chain(d):
                        G = D[d]
                        order = (2, 3, 0, 1) if d == 0 else (3, 2, 1, 0)
                        H = G["H"]
                        R_, U_ = G["RU"]
                        tH = [dve(lambda e: e.memset(H, 0.0))]
                        for i, q_ in enumerate(order):
                            sl = slice(128 * q_, 128 * q_ + 128)
                            ps, fr = PM.take()
                            mm(ps[:, 0:128], G["KK"][:, sl], H, True, False, tH, fr, G["tAK"])
                            for e_ in range(2):
                                t = mm(ps[:, 64 * e_:64 * e_ + 64], G["AK"][:, 512 * e_ + 128 * q_:512 * e_ + 128 * q_ + 128],
                                       Vt[:, q_, 64 * e_:64 * e_ + 64], False, e_ == 1, tV)
                            t = acp(R_, ps[:, 0:128], t)
                            yield
                            for e_ in range(2):
                                t2 = mm(ps[:, 128 + 64 * e_:192 + 64 * e_], G["XT"][:, 512 * e_ + 128 * q_:512 * e_ + 128 * q_ + 128],
                                        R_[:, 64 * e_:64 * e_ + 64], True, True, t, G["tinv"])
                            t2 = acp(U_, ps[:, 128:256], t2)
                            PM.give(ps, t2)
                            yield
                            if q_ < 2:
                                ps, fr = PM.take()
                                mm(ps[:, 0:128], H, G["Rd"][:, sl], True, False, t2, fr, G["tRK"], G["tRB"])
                                for e_ in range(2):
                                    o = ps[64 * e_:64 * e_ + 64, 0:128]
                                    ua = slice(256 * e_ + 128 * q_, 256 * e_ + 128 * q_ + 128)
                                    mm(o, Vt[:, q_, 64 * e_:64 * e_ + 64], G["RK"][:, ua], False, False)
                                    t3 = mm(o, U_[:, 64 * e_:64 * e_ + 64], G["RB"][:, ua], False, True)
                                ty = acp(G["Y"][:, sl], ps[:, 0:128], t3)
                                PM.give(ps, ty)
                                G["tY"] = ty
                            if i < 3:
                                ps, fr = PM.take()
                                mm(ps[:, 0:128], ident, H, True, False, fr, tH)
                                mm(ps[:, 0:128], G["Kt"][:, sl], Vt[:, q_, :], False, False, G["tKt"])
                                t4 = mm(ps[:, 0:128], G["Bt"][:, sl], U_, False, True, t2, G["tBt"])
                                tH = [acp(H[64 * e_:64 * e_ + 64, 64 * e_:64 * e_ + 64], ps[64 * e_:64 * e_ + 64, 64 * e_:64 * e_ + 64], t4, G["tes"],
                                          scale=G["es"][64 * e_:64 * e_ + 64, q_:q_ + 1]) for e_ in range(2)]
                                PM.give(ps, *tH)
                            yield

                    def whole(d, tin):
                        yield from scores(d, tin)
                        G = D[d]
                        G["tinv"] = yield from inverse(d, G["NA"], G["tNA"], G["X"], G["XT"], G["Q"], G["qf"], [prev_done, G["tsc"]])
                        yield from chain(d)
                    b0, ti0 = prep(0)
                    b1, ti1 = prep(1)
                    gens = [whole(0, ti0), whole(1, ti1)]
                    while gens:
                        al = []
                        for g in gens:
                            try:
                                next(g)
                                al.append(g)
                            except StopIteration:
                                pass
                        gens = al
                        yield
                    y, s_ = ys[0:2]
                    t = tt(y, D[0]["Y"], D[1]["Y"], add, D[0]["tY"], D[1]["tY"])
                    ps, fr = PM.take()
                    t1 = mm(ps[:, 0:256], bones, y, True, True, t, fr)
                    t = stt(y, ps[:, 0:256], -1.0 / 64, y, mult, add, t1)
                    t1 = af(s_, y, ACT.Square, t)
                    PM.give(ps, t)
                    ps, t, _ = rsq(s_, 2, 1.0 / 64, 64e-5, t1)
                    t = tt(y, y, ps[:, 0:256], mult, t)
                    PM.give(ps, t)
                    t = ts(y, y, P("lnw", c, 1), P("lnb", c, 1), mult, add)
                    t = tt(s_, psb[:, 0:256], vT[:, 0:256], mult, b1)
                    PM.give(psb, t)
                    t = tt(y, y, s_, add)
                    ps, fr = PM.take()
                    for m in range(2):
                        t1 = mm(ps[:, 0:256], L6[:, 4 + m, :], sg[:, m, :], m == 0, m == 1, fr, T[("sg", 0)], T[("sg", 1)], tl)
                    t = tt(ya[:, c, :], y, ps[:, 0:256], mult, t, t1)
                    PM.give(ps, t)
                    loq[0] = t
                    if c < 7:
                        lload(c + 1)
                    tyl.append(t)
                    prev_done = barrier()
                    yield
            w0h = alloc(16)
            a0h = alloc(16)
            ts(w0h, P("w0"), 0.5, None, mult, None, bar)
            twh = ts(a0h, P("a0"), 0.5, None, mult, None, bar)
            run(branch_a())
            if upto == 3:
                for c in range(8):
                    t = acp(xT[:, c, :], ya[:, c, :], tyl)
                return [t]

            at[0] = mark2
            bar = barrier()
            yb = alloc(2048).rearrange("p (k t) -> p k t", k=8)
            mark3 = at[0]
            gb = {k: alloc(64).rearrange("p (q n) -> p q n", q=4) for k in ("g", "beta", "nbeta", "gc", "egc", "negc", "gt", "egt", "eend", "tmp", "tmp2")}
            ea = alloc(16)
            t = af(ea, P("alog"), ACT.Exp, bar)
            tea = t
            av = ab[:, :, 0:16]
            bv = ab[:, :, 16:32]
            t = tt(gb["g"], av, bc(P("dtb"), 4), add, T["ab"], bar)
            t = af(gb["tmp"], gb["g"], ACT.Abs, t)
            t = af(gb["tmp"], gb["tmp"], ACT.Exp, t, scale=-1.0)
            t = af(gb["tmp"], gb["tmp"], ACT.Ln, t, bias=1.0)
            t = stt(gb["g"], gb["g"], 0.0, gb["tmp"], ALU.max, add, t)
            t = stt(gb["g"], gb["g"], -1.0, bc(ea, 4), mult, mult, t, tea)
            tg = t
            t = af(gb["beta"], bv, ACT.Tanh, T["ab"], bar, scale=0.5)
            t = ts(gb["beta"], gb["beta"], 0.5, 0.5, mult, add, t)
            tbeta = ts(gb["nbeta"], gb["beta"], -1.0, None, mult, None, t)
            ps, fr = PM.take()
            p3 = ps[:, 0:64].rearrange("p (q n) -> p q n", q=4)
            p4_ = ps[:, 64:128].rearrange("p (q n) -> p q n", q=4)
            for d in range(2):
                for q_ in range(4):
                    t = mm(p3[:, q_, 8 * d:8 * d + 8], C("LE" if d == 0 else "GE"), gb["g"][:, q_, 8 * d:8 * d + 8], True, True, tg, fr)
            for q_ in range(4):
                t = mm(p4_[:, q_, :], ones, gb["g"][:, q_, :], True, True)
            t1 = af(gb["egc"], p3, ACT.Exp, t)
            t = acp(gb["gc"], p3, t)
            t = tt(gb["gt"], p4_, gb["gc"], sub, t)
            t1 = af(gb["eend"], gb["gt"], ACT.Exp, t)
            t1 = af(gb["egt"], p4_, ACT.Exp, t)
            PM.give(ps, t1)
            tgb = ts(gb["negc"], gb["egc"], -1.0, None, mult, None, t1)

            kraw = alloc(512)
            HB = []
            for d in range(2):
                HB.append(dict(NA=alloc(512), AT=alloc(256), X=alloc(512), XT=alloc(512), Q=[alloc(512) for _ in range(2)],
                               S=alloc(128), RU=[alloc(128) for _ in range(2)], dec=alloc(512), gl=alloc(512),
                               qs=alloc(256), Ke=alloc(512), O=alloc(256), qf=[None, None]))
            kb = alloc(512)
            vb = alloc(512)
            qb_ = alloc(256)
            gzb = alloc(256)
            kt_ = alloc(512)
            vt_ = alloc(512)
            t1b = alloc(512)
            t2b = alloc(512)
            for d in range(2):
                for qb in HB[d]["Q"]:
                    tq0 = pool(lambda e, qb=qb: e.tensor_copy(qb.rearrange("p (u s) -> p u s", u=4), bc(ident, 4)), bar)
                HB[d]["qf"] = [tq0, tq0]
            tyb = []

            def branch_b():
                prev = bar
                for h in range(8):
                    E = {}

                    def ev_conv(dst, n, key, N):
                        def f(ps, t):
                            segs = N // 256
                            t0 = acp(kraw[:, 0:N], ps[:, 0:N], t, prev, E.get("rawf"))
                            zv = kraw[:, 0:N].rearrange("p (s t) -> p s t", s=segs)
                            w_ = t1b[:, 0:N]
                            wv = w_.rearrange("p (s t) -> p s t", s=segs)
                            t1 = ts(w_, kraw[:, 0:N], P("conv", 24 + n, 1), None, mult, None, t0, E.get("rawf"), prev)
                            t1 = stt(wv[:, :, 1:256], zv[:, :, 0:255], P("conv", n, 1), wv[:, :, 1:256], mult, add)
                            t1 = stt(wv[:, :, 0:255], zv[:, :, 1:256], P("conv", 48 + n, 1), wv[:, :, 0:255], mult, add)
                            t2 = af(t2b[:, 0:N], w_, ACT.Tanh, t1, scale=0.5)
                            E[key] = stt(dst, t2b[:, 0:N], 1.0, w_, add, mult, t2, prev)
                            E["rawf"] = E[key]
                            return [t0]
                        return f
                    yield from project(0, 256, hT, th, ev_conv(qb_, h, "q", 256))
                    yield from project(0, 512, hT, th, ev_conv(kb, 8 + h, "k", 512))
                    yield from project(0, 512, hT, th, ev_conv(vb, 16 + h, "v", 512))

                    def ev_gz(ps, t):
                        t0 = af(gzb, ps[:, 0:256], ACT.Tanh, t, prev, scale=0.5)
                        E["gz"] = stt(gzb, gzb, 1.0, ps[:, 0:256], add, mult, t0)
                        return [E["gz"]]
                    yield from project(0, 256, hT, th, ev_gz)
                    tsq = None
                    for buf, N, fac, key in ((qb_, 256, 0.5 * 128 ** -0.5, "q"), (kb, 512, 0.5, "k")):
                        t = af(t2b[:, 0:N], buf, ACT.Square, E[key], E["v"], tsq)
                        ps, t, tsq = rsq(t2b[:, 0:N], 1, 0.25, 1e-12, t)
                        E[key] = stt(buf, buf, fac, ps[:, 0:N], mult, mult, t)
                        PM.give(ps, E[key])
                    for src, dst, key, sc0 in ((kb, kt_, "kt", 1.0), (vb, vt_, "vt", 0.5)):
                        ps, fr = PM.take()
                        for q_ in range(4):
                            t = tr(ps[:, 128 * q_:128 * q_ + 128], src[:, 128 * q_:128 * q_ + 128], E["k"], E["v"], fr)
                        E[key] = acp(dst, ps, t, prev, scale=sc0)
                        PM.give(ps, E[key])
                    yield

                    def whole(d):
                        G = HB[d]
                        col = 8 * d + h
                        a_m, b_m = ("GT", "LE") if d == 0 else ("LT", "GE")
                        for q_ in range(4):
                            t = ts(G["gl"][:, 128 * q_:128 * q_ + 128], C(a_m), gb["g"][:, q_, col:col + 1], None, mult, None, prev)
                        ps, fr = PM.take()
                        for q_ in range(4):
                            t1 = mm(ps[:, 128 * q_:128 * q_ + 128], G["gl"][:, 128 * q_:128 * q_ + 128], C(b_m), True, True, t, fr)
                        td = af(G["dec"], ps, ACT.Exp, t1, prev)
                        PM.give(ps, td)
                        yield
                        for q_ in range(4):
                            sl = slice(128 * q_, 128 * q_ + 128)
                            tke = acp(G["Ke"][:, sl], kt_[:, sl], E["kt"], prev, tgb, scale=gb["eend"][:, q_, col:col + 1])
                        tds = ptt(G["gl"].rearrange("p (u t) -> p u t", u=4), G["dec"].rearrange("p (u t) -> p u t", u=4),
                                  bc(C("strict", 128 * d, 128), 4), mult, td, t1)
                        ps, fr = PM.take()
                        for q_ in range(4):
                            sl = slice(128 * q_, 128 * q_ + 128)
                            t1 = mm(ps[:, sl], kb[:, sl], kb[:, sl], True, True, E["k"], fr)
                        for q_ in range(4):
                            sl = slice(128 * q_, 128 * q_ + 128)
                            t1 = stt(G["NA"][:, sl], G["gl"][:, sl], gb["nbeta"][:, q_, col:col + 1], ps[:, sl], mult, mult, tds, t1, tbeta)
                        PM.give(ps, t1)
                        tNA = t1
                        yield
                        ps, fr = PM.take()
                        for q_ in range(2):
                            sl = slice(128 * q_, 128 * q_ + 128)
                            t1 = mm(ps[:, sl], kb[:, sl], qb_[:, sl], True, True, E["q"], fr)
                        for q_ in range(2):
                            t2 = mm(ps[:, 256 + 128 * q_:384 + 128 * q_], gb["g"][:, q_, col:col + 1].broadcast_to([128, 128]), C(b_m), True, True)
                        tdi = ptt(G["dec"][:, 0:256].rearrange("p (u t) -> p u t", u=2), G["dec"][:, 0:256].rearrange("p (u t) -> p u t", u=2),
                                  bc(C("incl", 128 * d, 128), 2), mult, tds)
                        tat = tt(G["AT"], G["dec"][:, 0:256], ps[:, 0:256], mult, t2, tdi, prev)
                        te = af(G["qs"], ps[:, 256:512], ACT.Exp, t2, prev, tat)
                        PM.give(ps, tat, te)
                        tqs = tt(G["qs"], G["qs"], qb_, mult, te)
                        yield
                        tinv = yield from inverse(d, G["NA"], tNA, G["X"], G["XT"], G["Q"], G["qf"], prev, U=4)
                        order = (2, 3, 0, 1) if d == 0 else (3, 2, 1, 0)
                        S = G["S"]
                        R_, U_ = G["RU"]
                        tS = dve(lambda e: e.memset(S, 0.0), prev)
                        for i, q_ in enumerate(order):
                            sl = slice(128 * q_, 128 * q_ + 128)
                            ps, fr = PM.take()
                            t = mm(ps[:, 0:128], kb[:, sl], S, True, True, tS, fr)
                            t = stt(R_, ps[:, 0:128], gb["negc"][:, q_, col:col + 1], vt_[:, sl], mult, add, t, E["vt"], tgb)
                            yield
                            t = mm(ps[:, 128:256], G["XT"][:, sl], R_, True, True, t, tinv)
                            tU = acp(U_, ps[:, 128:256], t, scale=gb["beta"][:, q_, col:col + 1])
                            PM.give(ps, tU)
                            yield
                            if q_ < 2:
                                ps, fr = PM.take()
                                mm(ps[:, 0:128], S, G["qs"][:, sl], True, False, tqs, tU, fr)
                                t = mm(ps[:, 0:128], U_, G["AT"][:, sl], False, True, tat)
                                G["tO"] = acp(G["O"][:, sl], ps[:, 0:128], t)
                                PM.give(ps, G["tO"])
                            if i < 3:
                                ps, fr = PM.take()
                                t = mm(ps[:, 0:128], G["Ke"][:, sl], U_, True, True, tke, tU, fr)
                                tS = stt(S, S, gb["egt"][:, q_, col:col + 1], ps[:, 0:128], mult, add, t)
                                PM.give(ps, tS)
                            yield
                    gens = [whole(0), whole(1)]
                    while gens:
                        al = []
                        for g in gens:
                            try:
                                next(g)
                                al.append(g)
                            except StopIteration:
                                pass
                        gens = al
                        yield
                    y = HB[0]["O"]
                    t = tt(y, y, HB[1]["O"], add, HB[0]["tO"], HB[1]["tO"])
                    t = af(t2b[:, 0:256], y, ACT.Square, t)
                    ps, t, _ = rsq(t2b[:, 0:256], 1, 1.0 / 128, EPS, t)
                    t = stt(y, y, P("gnw"), ps[:, 0:256], mult, mult, t)
                    PM.give(ps, t)
                    t = stt(yb[:, h, :], y, 0.5, gzb, mult, mult, t, E["gz"])
                    tyb.append(t)
                    prev = barrier()
                    yield
            run(branch_b())
            if upto == 4:
                for c in range(8):
                    t = acp(xT[:, c, :], yb[:, c, :], tyb)
                return [t]

            at[0] = mark3
            bar = barrier()
            tback = Q.dma(xT_[:, :], XS, "back", bar)
            mg = alloc(4096).rearrange("p (k t) -> p k t", k=16)
            ga = Ring([alloc(256) for _ in range(2)])
            gbb = Ring([alloc(256) for _ in range(2)])
            tmg = []

            def merges():
                for c in range(16):
                    E = {}
                    for nm, ring in (("a", ga), ("b", gbb)):
                        buf, fb_ = ring.take()

                        def f(ps, t, buf=buf, fb_=fb_, nm=nm):
                            t0 = af(buf, ps, ACT.Tanh, t, fb_, bar, scale=0.5)
                            E[nm] = t0
                            E[nm + "b"] = buf
                            return [t0]
                        yield from project(0, 256, hT, th, f)
                    w, tw, s = wtake()
                    ps, fr = PJ.take()
                    for k in range(8):
                        t = mm(ps[:, 0:256], w[:, k, :], ya[:, k, :], k == 0, k == 7, tw, fr, tyl)
                    for k in range(8):
                        t = mm(ps[:, 256:512], w[:, 8 + k, :], yb[:, k, :], k == 0, k == 7, tyb)
                    wgive(s, t)
                    t1 = stt(E["ab"], E["ab"], 1.0, ps[:, 0:256], add, mult, t, E["a"])
                    t2 = stt(E["bb"], E["bb"], 1.0, ps[:, 256:512], add, mult, E["b"])
                    PJ.give(ps, t2)
                    t3 = tt(mg[:, c, :], E["ab"], E["bb"], add, bar)
                    ga.give(E["ab"], t3)
                    gbb.give(E["bb"], t3)
                    tmg.append(t3)
                    yield
            run(merges())
            g1h = alloc(16)
            tgh = ts(g1h, mod[:, 32:48, 0], 0.5, None, mult, None, bar)
            txl = []

            def ev_x(c, gate):
                def f(ps, t):
                    t = stt(xT[:, c, :], ps, gate, xT[:, c, :], mult, add, t, tgh, tback)
                    txl.append(t)
                    return [t]
                return f
            run((x for c in range(16) for x in project(0, 256, mg, tmg, ev_x(c, g1h[:, c:c + 1]))))

            at[0] = mark
            bar = barrier()
            sq = alloc(2048).rearrange("p (g k t) -> p g k t", g=2, k=4)
            h2 = hT.rearrange("p k t -> p (k t)")[:, 0:4096].rearrange("p (k t) -> p k t", k=16)
            u = alloc(64 * 256 - 4096)
            ulo = hT.rearrange("p k t -> p (k t)")[:, 4096:8192].rearrange("p (k t) -> p k t", k=16)
            uhi = u.rearrange("p (k t) -> p k t", k=48)

            def uk(k):
                return ulo[:, k, :] if k < 16 else uhi[:, k - 16, :]
            t = norm_scale(xT, rb[:, 0:256], sq, txl, bar)
            for k in range(16):
                t = stt(h2[:, k, :], xT[:, k, :], A_[:, 2, k:k + 1], rb[:, 0:256], mult, mult, t, bar)
                ta = af(h2[:, k, :], h2[:, k, :], ACT.Identity, t, bias=mod[:, 48 + k, 0:1])
            th2 = ta
            tu = []

            def ev_u(k):
                def f(ps, t):
                    t0 = af(uk(k), ps, ACT.Relu, t, bar)
                    tu.append(pool(lambda e: e.tensor_tensor(uk(k), uk(k), uk(k), mult), t0))
                    return [t0]
                return f
            run((x for k in range(64) for x in project(0, 256, h2, th2, ev_u(k))))
            txn = []
            for c in range(16):
                ps, fr = PJ.take()
                for g in range(4):
                    w, tw, s = wtake()
                    for k in range(16):
                        t = mm(ps[:, 0:256], w[:, k, :], uk(16 * g + k), g == 0 and k == 0, g == 3 and k == 15, tw, fr, tu[16 * g + k])
                    wgive(s, t)
                t = stt(xT[:, c, :], ps[:, 0:256], mod[:, 80 + c, 0:1], xT[:, c, :], mult, add, t, th2)
                PJ.give(ps, t)
                txn.append(t)
            return txn

        t = [tx, tnh]
        if upto >= 1:
            t = layer(0, t)
        if upto >= 2:
            t = layer(1, t)
            t = final_norm(t, "fng")
        if upto >= 3:
            t = second(t)
        if upto >= 5:
            t = final_norm(t, "fnw")
        store(t)

        totals = Q.number()
        sem = {s: ctx.enter_context(nc.semaphore("s_" + s)) for s in totals}
        block = ctx.enter_context(nc.Block())

        @block.sync
        def _(e):
            Q.play("s", e, sem, totals)

        @block.tensor
        def _(e):
            Q.play("t", e, sem, totals)

        @block.vector
        def _(e):
            Q.play("v", e, sem, totals)

        @block.scalar
        def _(e):
            Q.play("a", e, sem, totals)

        @block.gpsimd
        def _(e):
            Q.play("p", e, sem, totals)


SEG = {}


def _segments():
    o = 0
    for n, w in (("fq", 512), ("fk", 512), ("fv", 512), ("ff", 4), ("fg", 512), ("dq", 512), ("dk", 512), ("dv", 512),
                 ("dg", 512), ("mq", 512), ("mk", 512), ("mv", 512), ("mg", 512), ("gq", 256), ("gk", 256), ("gv", 512),
                 ("ga", 16), ("gg", 512)):
        SEG[n] = (o, w)
        o += w


_segments()


def layout(inp):
    g = {k: np.asarray(v) for k, v in inp.items()}
    W = np.empty((NT, 128, 16, 128), np.float32)
    n = [0]

    def tiles(w):
        k = w.shape[0] // 128
        m = w.shape[1] // 128
        v = w.reshape(k, 128, m, 128).transpose(2, 1, 0, 3)
        if k == 16:
            W[n[0]:n[0] + m] = v
            n[0] += m
        elif k == 64:
            v = v.reshape(m, 128, 4, 16, 128).transpose(0, 2, 1, 3, 4)
            W[n[0]:n[0] + 4 * m] = v.reshape(4 * m, 128, 16, 128)
            n[0] += 4 * m

    wsm = np.empty((2, 128, 320), np.float32)
    for l in range(2):
        w = g["w_in"][l]
        for nm in ("fq", "fk", "fv", "fg", "dq", "dk", "dv", "dg", "mq", "mk", "mv", "mg", "gq", "gk", "gv", "gg"):
            o, wd = SEG[nm]
            tiles(w[:, o:o + wd])
        sm = np.concatenate([w[:, SEG["ff"][0]:SEG["ff"][0] + 4], w[:, SEG["ga"][0]:SEG["ga"][0] + 16]], 1)
        wsm[l] = sm.reshape(16, 128, 20).transpose(1, 0, 2).reshape(128, 320)
        tiles(g["w_out"][l])
    tiles(g["mod_w_2"][0])
    w = g["in_w_2"][0]
    AC = 3552
    tiles(np.concatenate([w[:, 3072:3168], w[:, AC + 4096:AC + 4128]], 1))
    tiles(w[:, 3168:3296])
    tiles(w[:, 3296:3552])
    for c in range(8):
        for j in range(3):
            tiles(w[:, 1024 * j + 128 * c:1024 * j + 128 * c + 128])
    for c in range(8):
        for j in range(4):
            tiles(w[:, AC + 1024 * j + 128 * c:AC + 1024 * j + 128 * c + 128])
    G0 = AC + 4128
    ua, ub = g["up_a_2"][0], g["up_b_2"][0]
    uab = np.concatenate([ua, ub], 0)
    for c in range(16):
        tiles(w[:, G0 + 128 * c:G0 + 128 * c + 128])
        tiles(w[:, G0 + 2048 + 128 * c:G0 + 2048 + 128 * c + 128])
        tiles(uab[:, 128 * c:128 * c + 128])
    tiles(g["out_w_2"][0])
    tiles(g["mlp_w1_2"][0])
    tiles(g["mlp_w2_2"][0])
    assert n[0] == NT, (n[0], NT)

    par = np.zeros((128, PARN), np.float32)

    def put(name, v, i=0):
        o = PAR[name][0] + i
        par[:v.shape[0], o:o + v.shape[1]] = v

    def col(v):
        return v.reshape(-1, 128).T

    def rep(v):
        return np.broadcast_to(v.reshape(1, -1), (128, v.size))
    for l in range(2):
        put("ng", col(g["norm_g"][l]), 16 * l)
        put("fb", rep(g["fox_fb"][l]), 4 * l)
        put("lam", g["diff_lam"][l].T, 4 * l)
        put("dng", col(g["diff_norm_g"][l]), l)
        put("gng", col(g["gla_norm_g"][l]), l)
        put("gba", col(g["gla_ba"][l]), 2 * l)
        put("wa2", g["gla_wa2"][l], 256 * l)
    put("fng", col(g["final_norm_g"]))
    cc = np.stack([col(g["c_2"][0]), col(g["c_ctx_2"])], 2)
    put("c", cc.reshape(128, 32))
    put("modb", col(g["mod_b_2"][0]))
    put("n1", col(g["norm1_w_2"][0]))
    put("n2", col(g["norm2_w_2"][0]))
    mu = g["rwkv_mu_2"][0]
    put("mu", col(mu[0:3072]))
    put("mu", mu[3072:3168].reshape(96, 1), 24)
    put("mu", col(mu[3168:3552]), 25)
    for d in range(2):
        put("w0", col(g["rwkv_w0_2"][0, d]), 8 * d)
        put("a0", col(g["rwkv_a0_2"][0, d]), 8 * d)
    put("kk", col(g["rwkv_k_k_2"][0]))
    put("ka", col(g["rwkv_k_a_2"][0]))
    put("rk", col(g["rwkv_r_k_2"][0].reshape(-1)))
    put("lnw", col(g["rwkv_ln_w_2"][0]))
    put("lnb", col(g["rwkv_ln_b_2"][0]))
    for k in range(3):
        put("conv", col(g["gdn_conv_w_2"][0, k]), 24 * k)
    put("alog", rep(g["gdn_a_log_2"][0]))
    put("dtb", rep(g["gdn_dt_bias_2"][0]))
    put("gnw", col(g["gdn_norm_w_2"][0]))
    put("fnw", col(g["final_norm_w_2"]))

    lora = np.zeros((8, 128, 6, 128), np.float32)
    for c in range(8):
        cs = slice(128 * c, 128 * c + 128)
        for d in range(2):
            lora[c, 0:96, d] = g["rwkv_w_up_2"][0, d][:, cs]
            lora[c, :, 2 + d] = g["rwkv_a_up_2"][0, d][:, cs]
            lora[c, :, 4 + d] = g["rwkv_g_up_2"][0][128 * d:128 * d + 128, cs]

    def chan(v):
        return np.ascontiguousarray(v[0].T.reshape(16, 128, 256).transpose(1, 0, 2).reshape(128, 4096))
    cst, mk = constants()
    return {"w": W.reshape(NT, 128, 2048), "wsm": wsm, "lora": lora.reshape(8, 128, 768), "par": par, "cst": cst, "msk": mk.view(np.uint32),
            "ctx": chan(g["ctx_2"]), "x": chan(g["x"])}


def build(nc, arrays, upto=99):
    aps = {}
    for k, v in arrays.items():
        aps[k] = nc.dram_tensor("in_" + k, v.shape, mybir.dt.from_np(v.dtype), kind="ExternalInput").ap()
    out = nc.dram_tensor("out_0", (128, 4096), F32, kind="ExternalOutput").ap()
    xs = nc.dram_tensor("x_kept", (128, 4096), F32, kind="Internal").ap()
    program(nc, aps["w"], aps["wsm"], aps["lora"], aps["par"], aps["cst"], aps["msk"], aps["ctx"], aps["x"], xs, out, upto)


def kernel(**inputs):
    import concourse.bacc as _bacc
    from concourse.bass_utils import run_bass_kernel_spmd as _run

    nc = _bacc.Bacc("TRN2", target_bir_lowering=False, num_devices=1)
    arrays = layout(inputs)
    build(nc, arrays)
    r = _run(nc, [{"in_" + k: v for k, v in arrays.items()}], core_ids=[0])
    o = r.results[0]["out_0"]
    return o.reshape(128, 16, 256).transpose(2, 1, 0).reshape(1, 256, 2048)
```

```python
import concourse.bass as bass
from concourse import mybir
from collections import deque
from contextlib import ExitStack
import math
import numpy as np

F32 = mybir.dt.float32
FR = mybir.dt.float32r
U8 = mybir.dt.uint8
ALU = mybir.AluOpType
ACT = mybir.ActivationFunctionType
AX = mybir.AxisListType

NW1 = 60
NWO = 16
NMOD = 96
NIN = 24 + 1 + 1 + 2 + 32 + 32
NT = 2 * (NW1 + NWO) + NMOD + NIN + 16 + 16 + 64 + 64
EPS = 1e-6
NSLOT = 3
MAXSLOT = 5

PAR = {}
PARN = 0
for _n, _w in (("ng", 32), ("fb", 8), ("lam", 8), ("dng", 2), ("gng", 2), ("gba", 4), ("wa2", 512), ("fng", 16),
               ("c", 32), ("modb", 96), ("n1", 16), ("n2", 16), ("mu", 28), ("w0", 16), ("a0", 16), ("kk", 8),
               ("ka", 8), ("rk", 8), ("lnw", 8), ("lnb", 8), ("conv", 72), ("alog", 16), ("dtb", 16), ("gnw", 1),
               ("fnw", 16)):
    PAR[_n] = (PARN, _w)
    PARN += _w

CST = {}
CSTN = 0
for _n, _w in (("ident", 128), ("ones", 128), ("bones", 128), ("LE", 128), ("GT", 128), ("GE", 128), ("LT", 128),
               ("G1", 256), ("mask3", 384), ("permd", 128), ("permm", 128), ("Cd", 256), ("Sd", 256), ("Cm", 256),
               ("Sm", 256), ("scan", 512), ("type", 6), ("strict", 256), ("incl", 256)):
    CST[_n] = (CSTN, _w)
    CSTN += _w
MSK = {"strict": (0, 256), "incl": (256, 256), "lev": (512, 896), "xt0": (1408, 128), "gla": (1536, 1024)}
MSKN = 2560


def constants():
    i = np.arange(128)
    a, b = i[:, None], i[None, :]
    c = np.zeros((128, CSTN), np.float32)

    def put(name, v):
        o, w = CST[name]
        c[:, o:o + w] = v

    put("ident", a == b)
    put("ones", 1.0)
    put("bones", (a // 64) == (b // 64))
    put("LE", a <= b)
    put("GT", a > b)
    put("GE", a >= b)
    put("LT", a < b)
    put("G1", np.concatenate([np.ones((128, 128)), a > b], 1))
    tri = np.where(b > a, np.float32(-1e30), np.float32(0.0))
    put("mask3", np.concatenate([tri, np.zeros((128, 128)), tri], 1))
    t = np.arange(256, dtype=np.float32)
    for nm, rot, width, pn in (("d", 16, 64, "permd"), ("m", 32, 128, "permm")):
        half = rot // 2
        inv = (np.float32(500000.0) ** (-np.arange(0, rot, 2, dtype=np.float32) / np.float32(rot))).astype(np.float32)
        ang = t[None, :] * inv[:, None]
        C = np.ones((128, 256), np.float32)
        S = np.zeros((128, 256), np.float32)
        L = np.zeros((128, 128), np.float32)
        for base in range(0, 128, width):
            for q in range(half):
                C[base + q] = C[base + half + q] = np.cos(ang[q])
                S[base + q] = S[base + half + q] = np.sin(ang[q])
                L[base + half + q, base + q] = -1.0
                L[base + q, base + half + q] = 1.0
        put("C" + nm, C)
        put("S" + nm, S)
        put(pn, L)
    sc = np.ones(512)
    sc[::128] = 0
    put("scan", sc[None, :])
    ty = np.zeros((128, 6))
    for q in range(4):
        ty[:, q] = i % 4 == q
    for q in range(2):
        ty[:, 4 + q] = i % 2 == q
    put("type", ty)
    st = np.concatenate([a < b, a > b], 1)
    inc = np.concatenate([a <= b, a >= b], 1)
    put("strict", st)
    put("incl", inc)
    m = np.zeros((128, MSKN), np.uint8)
    m[:, 0:256] = st
    m[:, 256:512] = inc
    j = np.arange(64)
    for d in range(2):
        for lv in range(7):
            w = 1 << lv
            s = (j // w) * 2 * w + d * w + j % w
            ok = (i[:, None] // (2 * w) == s[None, :] // (2 * w)) & ((i[:, None] // w) % 2 != (s[None, :] // w) % 2)
            m[:, 512 + (d * 7 + lv) * 64:512 + (d * 7 + lv) * 64 + 64] = ok
        tcol = 2 * j + 1 - d
        m[:, 1408 + d * 64:1408 + d * 64 + 64] = (i[:, None] // 2 == tcol[None, :] // 2) & (i[:, None] != tcol[None, :])
    for lv in range(7):
        w = 1 << lv
        m[:, 1536 + lv * 128:1536 + lv * 128 + 128] = (a // (2 * w) == b // (2 * w)) & ((a // w) % 2 == 0) & ((b // w) % 2 == 1)
    m[:, 1536 + 896:1536 + 1024] = a == b
    return c, m


class Tok:
    __slots__ = ("sem", "val", "need", "inc")

    def __init__(self, sem, inc=1):
        self.sem, self.val, self.need, self.inc = sem, None, False, inc


class Queues:

    def __init__(self):
        self.ops = {k: [] for k in ("t", "v", "a", "p", "s")}
        self.last = {}
        self.sems = {}

    def add(self, eng, fn, after, sem=None):
        tok = Tok(sem or eng, 16 if sem else 1)
        waits = []

        def flat(x):
            if x is None:
                return
            if isinstance(x, Tok):
                x.need = True
                waits.append(x)
            else:
                for y in x:
                    flat(y)
        flat(after)
        if eng in "vap" and not sem:
            if eng in self.last:
                flat(self.last[eng])
            self.last[eng] = tok
        self.ops[eng].append((waits, fn, tok))
        return tok

    def pe(self, fn, *after):
        return self.add("t", fn, after)

    def dve(self, fn, *after):
        return self.add("v", fn, after)

    def act(self, fn, *after):
        return self.add("a", fn, after)

    def pool(self, fn, *after):
        return self.add("p", fn, after)

    def dma(self, out, in_, sem, *after):
        return self.add("s", lambda e: e.dma_start(out, in_), after, sem)

    def number(self):
        count = {}
        for eng in self.ops:
            for _, _, tok in self.ops[eng]:
                if tok.need or tok.inc == 16:
                    count[tok.sem] = count.get(tok.sem, 0) + tok.inc
                    tok.val = count[tok.sem]
        return count

    def play(self, eng, e, sem, totals):
        seen = {}
        for waits, fn, tok in self.ops[eng]:
            top = {}
            for w in waits:
                top[w.sem] = max(top.get(w.sem, 0), w.val)
            for s, v in top.items():
                if seen.get(s, 0) < v:
                    e.wait_ge(sem[s], v)
                    seen[s] = v
            ins = fn(e)
            if tok.val is not None:
                ins.then_inc(sem[tok.sem], tok.inc)
        if eng == "s":
            for s, v in totals.items():
                if s not in ("t", "v", "a", "p"):
                    e.wait_ge(sem[s], v)


class Ring:

    def __init__(self, aps):
        self.q = deque((x, ()) for x in aps)

    def take(self):
        return self.q.popleft()

    def give(self, ap, *toks):
        self.q.append((ap, toks))


def program(nc, W, WSM, LORA, PARd, CSTd, MSKd, CTX, XIN, XS, OUT, upto=99):
    Q = Queues()
    pe, dve, act, pool = Q.pe, Q.dve, Q.act, Q.pool
    ctx = ExitStack()
    with ctx:
        def sb(name, n, dt=F32):
            return ctx.enter_context(nc.sbuf_tensor(name, [128, n], dt))

        par = sb("par", PARN)
        cst = sb("cst", CSTN)
        msk = sb("msk", MSKN // 4, mybir.dt.uint32)
        msk8 = msk[:, :].bitcast(U8)
        nhalf = sb("nhalf", 1)
        smalls = sb("smalls", 48)
        mods = sb("mods", 304)
        xT_ = sb("xT", 16 * 256)
        wring = sb("wring", NSLOT * 2048)
        TOTAL = 37100
        cur = {}
        ctx.callback(lambda: cur["stack"].close())

        def scope(name, split, acts, slots=NSLOT):
            if cur:
                cur["stack"].close()
            st = ExitStack()
            n = TOTAL - split * 2048 - acts * 8192 - (slots - NSLOT) * 2048
            cur.clear()
            cur["stack"] = st
            cur["n"] = n
            cur["ring"] = [wring[:, i * 2048:(i + 1) * 2048] for i in range(NSLOT)]
            cur["ring"] += [st.enter_context(nc.sbuf_tensor(f"wring{i}_{name}", [128, 2048], F32))[:, :] for i in range(NSLOT, slots)]
            cur["arena"] = st.enter_context(nc.sbuf_tensor("arena_" + name, [128, n], F32))
            fr_ = [st.enter_context(nc.sbuf_tensor(f"part{i}_{name}", [128, 1024], FR))[:, :].rearrange("p (k n) -> p k n", k=8)
                   for i in range(2 * split)]
            cur["wh"] = Ring([(fr_[2 * i], fr_[2 * i + 1]) for i in range(split)])
            ac = [st.enter_context(nc.sbuf_tensor(f"act{i}_{name}", [128, 4096], FR))[:, :].rearrange("p (k t) -> p k t", k=16)
                  for i in range(2 * acts)]
            cur["acts"] = [(ac[2 * i], ac[2 * i + 1]) for i in range(acts)]
            cur["bar"] = barrier()
        banks = [ctx.enter_context(nc.psum_tensor(f"bank{i}", [128, 512], F32)) for i in range(8)]

        xT = xT_[:, :].rearrange("p (k t) -> p k t", k=16)

        def P(name, i=0, w=None):
            o, n = PAR[name]
            return par[:, o + i:o + i + (n if w is None else w)]

        def C(name, i=0, w=None):
            o, n = CST[name]
            return cst[:, o + i:o + i + (n if w is None else w)]

        def M(name, i=0, w=None):
            o, n = MSK[name]
            return msk8[:, o + i:o + i + (n if w is None else w)]

        ident = C("ident")
        ones = C("ones")
        bones = C("bones")

        def bc(ap, n):
            return ap[:, None, :].broadcast_to([ap.shape[0], n, ap.shape[1]])

        def bcl(ap, n):
            return ap[:, :, None].broadcast_to([ap.shape[0], ap.shape[1], n])

        at = [0]

        def alloc(n, **dims):
            a = cur["arena"][:, at[0]:at[0] + n]
            at[0] += n
            assert at[0] <= cur["n"] - cur.get("kept", 0), at[0]
            return a

        def barrier():
            return [Q.last.get("v"), Q.last.get("a"), Q.last.get("p"), Q.ops["t"][-1][2] if Q.ops["t"] else None]

        PJ = Ring([banks[i][:, :] for i in range(2)])
        PM = Ring([banks[i][:, :] for i in range(2, 8)])

        def mm(out, lhsT, rhs, start, stop, *after):
            return pe(lambda e: e.matmul(out, lhsT, rhs, start=start, stop=stop), *after)

        def tr(out, in_, *after):
            return pe(lambda e: e.transpose(out, in_, ident), *after)

        def tt(out, a, b, op, *after):
            return dve(lambda e: e.tensor_tensor(out, a, b, op), *after)

        def ts(out, a, s1, s2, op0, op1, *after):
            if s2 is None:
                return dve(lambda e: e.tensor_scalar(out, a, s1, None, op0), *after)
            return dve(lambda e: e.tensor_scalar(out, a, s1, s2, op0, op1), *after)

        def stt(out, a, s, b, op0, op1, *after):
            return dve(lambda e: e.scalar_tensor_tensor(out, a, s, b, op0, op1), *after)

        def af(out, a, func, *after, scale=1.0, bias=0.0):
            return act(lambda e: e.activation(out, a, func, scale=scale, bias=bias), *after)

        def acp(out, a, *after, scale=1.0):
            return act(lambda e: e.activation(out, a, ACT.Copy, scale=scale), *after)

        def ptt(out, a, b, op, *after):
            return pool(lambda e: e.tensor_tensor(out, a, b, op), *after)

        def cpred(out, mask, data, *after):
            return dve(lambda e: e.copy_predicated(out, mask, data), *after)

        mult, add, sub = ALU.mult, ALU.add, ALU.subtract

        l0 = [Q.dma(cst[:, :], CSTd, "ld0"), Q.dma(par[:, :], PARd, "ld1"), Q.dma(msk[:, :], MSKd, "ld2"),
              Q.dma(xT_[:, :], XIN, "ld3")]
        tx = l0[3]
        tnh = dve(lambda e: e.memset(nhalf[:, :], -0.5), l0)

        wfree = [()] * MAXSLOT
        wn = [0]
        nb1 = 2 * (NW1 + NWO)
        main_tiles = iter(list(range(nb1)) + list(range(nb1 + NMOD, NT)))
        mod_tiles = iter(range(nb1, nb1 + NMOD))

        def wtake(stream=main_tiles):
            i = next(stream)
            s = wn[0] % len(cur["ring"])
            wn[0] += 1
            ap = cur["ring"][s]
            t = Q.dma(ap, W[i], f"w{s}", wfree[s], cur["bar"] if s >= NSLOT else ())
            wfree[s] = None
            return ap.rearrange("p (k n) -> p k n", k=16), t, s

        def wgive(s, *toks):
            wfree[s] = toks

        smr = Ring([smalls[:, 8 * i:8 * i + 8] for i in range(6)])

        def root(sums, n, heads, c1, c2, t, release):
            sm, fs = yield from grab(smr)
            s_ = sm[:, 0:n]
            t = ts(s_, sums, c1, c2, mult, add, t, fs)
            release(t)
            t = pool(lambda e: e.tensor_tensor(s_, s_, nhalf[:, 0:1].broadcast_to([128, n]), ALU.pow), t, tnh)
            yield
            p2, fr2 = yield from grab(PM)
            w = 128 // heads
            for m in range(n // heads):
                for e_ in range(heads):
                    l_ = sm[:, heads * m + e_:heads * m + e_ + 1].broadcast_to([128, w])
                    t2 = mm(p2[w * e_:w * e_ + w, 128 * m:128 * m + 128], l_, ident, True, True, t, fr2)
            smr.give(sm, t2)
            yield
            return p2, t2

        def rsq(sq, heads, c1, c2, *after):
            n = sq.shape[1] // 128
            ps, fr = yield from grab(PM)
            rhs = bones[:, 0:128:64] if heads == 2 else ones[:, 0:1]
            for m in range(n):
                t = mm(ps[:, heads * m:heads * m + heads], sq[:, 128 * m:128 * m + 128], rhs, True, True, fr, *after)
            yield
            p2, t2 = yield from root(ps[:, 0:n * heads], n * heads, heads, c1, c2, t, lambda t: PM.give(ps, t))
            return p2, t2, t

        def value(g):
            while True:
                try:
                    next(g)
                except StopIteration as e:
                    return e.value

        def norm_scale(xs, rb, sq, *txs):
            ps, fr = PM.take()
            pq, fq = PM.take()
            for g in range(4):
                ta = af(sq[:, g % 2], xs[:, 4 * g:4 * g + 4, :], ACT.Square, txs, sqf[g % 2])
                for k in range(4):
                    mm(ps[:, 0:1], sq[:, g % 2, k, 0:128], ones[:, 0:1], g == 0 and k == 0, g == 3 and k == 3, ta, fr, fq)
                    t = mm(pq[:, 0:1], sq[:, g % 2, k, 128:256], ones[:, 0:1], g == 0 and k == 0, g == 3 and k == 3)
                sqf[g % 2] = t
            s2, f2 = smr.take()
            t = acp(s2[:, 0:1], ps[:, 0:1], t, f2)
            PM.give(ps, t)
            t = acp(s2[:, 1:2], pq[:, 0:1], t)
            PM.give(pq, t)
            p2, t2 = value(root(s2[:, 0:2], 2, 1, 1.0 / 2048, EPS, t, lambda t: smr.give(s2, t)))
            t2 = acp(rb, p2[:, 0:256], t2)
            PM.give(p2, t2)
            return t2

        sqf = [None, None]

        ready = deque()
        ahead = {"end": 0}
        plain_up = set(nb1 + 28 + 32 + 3 * c + 2 for c in range(16))
        pos = [0]

        def part(hi, lo, src, t, *after):
            t1 = acp(hi, src, t, *after)
            return tt(lo, src, hi.bitcast(F32), sub, t1)

        def fill(n):
            while len(ready) < n and pos[0] < ahead["end"]:
                if pos[0] in plain_up:
                    pos[0] += 1
                    ready.append(wtake())
                    continue
                if len(cur["wh"].q) == 0:
                    return
                if "tile" not in ahead:
                    ahead["tile"] = wtake()
                    ahead["half"] = 0
                w, tw, s = ahead["tile"]
                h = ahead["half"]
                (wh, wl), fw = cur["wh"].take()
                t1 = acp(wh, w[:, 8 * h:8 * h + 8, :], tw, fw, cur["bar"])
                t2 = tt(wl[:, 0:4, :], w[:, 8 * h:8 * h + 4, :], wh[:, 0:4, :].bitcast(F32), sub, t1)
                t3 = ptt(wl[:, 4:8, :], w[:, 8 * h + 4:8 * h + 8, :], wh[:, 4:8, :].bitcast(F32), sub, t1)
                ready.append((wh, wl, t2, t3))
                ahead["half"] += 1
                if h == 1:
                    wgive(s, t2, t3)
                    del ahead["tile"]
                    pos[0] += 1

        def products(ps, X, k0, th, fr, first, last):
            fill(1)
            wh, wl, t2, t3 = ready.popleft()
            for k in range(8):
                x = [X[j][:, k0 + k, :] for j in range(2)]
                tk_ = th[k0 + k] if isinstance(th, list) else th
                t = mm(ps, wh[:, k, :], x[0], first and k == 0, False, t2, t3, fr, tk_)
                t = mm(ps, wh[:, k, :], x[1], False, False)
                t = mm(ps, wl[:, k, :], x[0], False, last and k == 7)
                if k == 3:
                    yield
                    fill(2)
            cur["wh"].give((wh, wl), t)
            return t

        def project(ntok0, ntok1, hT, th, evac, step=4):
            if isinstance(hT, tuple):
                ps, fr = PJ.take()
                for half in range(2):
                    t = yield from products(ps[:, 0:256], hT, 8 * half, th, fr, half == 0, half == 1)
                    if half == 0:
                        yield
                PJ.give(ps, *evac(ps[:, 0:256], t))
                yield
                return
            w, tw, s = wtake()
            pos[0] += 1
            ps, fr = PJ.take()
            for k in range(16):
                t = mm(ps[:, 0:ntok1 - ntok0], w[:, k, :], hT[:, k, ntok0:ntok1], k == 0, k == 15, tw, fr, th[k] if isinstance(th, list) else th)
                if k % step == step - 1 and k < 15:
                    yield
            wgive(s, t)
            PJ.give(ps, *evac(ps[:, 0:ntok1 - ntok0], t))
            yield

        def together(*gens):
            said = [None] * len(gens)
            left = list(enumerate(gens))
            while left:
                alive = []
                for i, g in left:
                    try:
                        next(g)
                        alive.append((i, g))
                    except StopIteration as e:
                        said[i] = e.value
                left = alive
                yield
            return said

        spawned = []

        def run(*gens, behind=None):
            main = together(*gens)
            going = True
            rounds = 0
            while going or spawned:
                going = going and next(main, "end") != "end"
                for g in list(spawned):
                    if next(g, "end") == "end":
                        spawned.remove(g)
                rounds += 1
                if behind and rounds % 5 in (0, 2):
                    next(behind, None)

        def grab(ring):
            while not ring.q:
                yield
            return ring.take()

        def need(n):
            while len(PM.q) < n:
                yield

        mod = mods[:, 0:192].rearrange("p (n two) -> p n two", two=2)
        scv = mods[:, 192:224].rearrange("p (k two) -> p k two", two=2)
        tmodl = []

        def modulation():
            scr = mods[:, 224:256]
            t = af(scr, P("c"), ACT.Tanh, tnh, scale=0.5)
            t = stt(mods[:, 192:224], scr, 1.0, P("c"), add, mult, t)
            tsc = ts(mods[:, 192:224], mods[:, 192:224], 0.5, None, mult, None, t)
            cur["kept"] = 1024
            top = cur["n"]
            accs = [cur["arena"][:, top - 1024 + 512 * j:top - 512 + 512 * j] for j in range(2)]
            free = None
            for n in range(24):
                two = 2 if n < 8 else 1
                for g in range(4):
                    w, tw, s = wtake(mod_tiles)
                    wv = w.rearrange("p k n -> p (k n)").rearrange("p (k n) -> p k n", k=4)
                    for kk_ in range(4):
                        k = 4 * g + kk_
                        for j in range(two):
                            a_ = accs[j]
                            if k == 0:
                                t = ts(a_, wv[:, kk_, :], scv[:, k, j:j + 1], None, mult, None, tw, tsc, free)
                            else:
                                t = stt(a_, wv[:, kk_, :], scv[:, k, j:j + 1], a_, mult, add, tw)
                        if kk_ == 3:
                            wgive(s, t)
                        if kk_ % 2 == 1:
                            yield
                yield
                yield from need(3)
                ps, fr = PM.take()
                for j in range(two):
                    for q_ in range(4):
                        free = mm(ps[:, 4 * j + q_:4 * j + q_ + 1], accs[j][:, 128 * q_:128 * q_ + 128], ones[:, 0:1], True, True, t, fr)
                yield
                for j in range(two):
                    t2 = tt(mod[:, 4 * n:4 * n + 4, j], ps[:, 4 * j:4 * j + 4], P("modb", 4 * n, 4), add, free)
                PM.give(ps, t2)
                tmodl.append(t2)
        modgen = modulation()

        def layer(l, tx):
            at[0] = 0
            bar = barrier()
            SC = 128 ** -0.5
            LI = 0.8 - 0.6 * math.exp(-0.3 * l)
            ahead["end"] = (NW1 + NWO) * (l + 1)
            hT = cur["acts"][0]
            mix_ = alloc(4096)
            mix = mix_.rearrange("p (k t) -> p k t", k=16)
            rb = alloc(256)
            wsm_ = alloc(320)
            wsm = wsm_.rearrange("p (k n) -> p k n", k=16)
            sq = mix_[:, 0:2048].rearrange("p (g k t) -> p g k t", g=2, k=4)
            tws = Q.dma(wsm_, WSM[l], f"sm{l}", bar)
            tr_ = norm_scale(xT, rb, sq, tx, bar)
            fl = alloc(48).rearrange("p (a b) -> p a b", b=8)
            ft = fl[:, 0:1, :].rearrange("p a b -> p (a b)")
            aT = alloc(256)
            ps, fr = PM.take()
            pf = [(ps, fr), PM.take()]
            pa, fra = PM.take()
            raw = Ring([alloc(256) for _ in range(3)])
            hk = raw
            fill(2)
            th = []
            for k in range(16):
                h_, fh = hk.take()
                t = stt(h_, xT[:, k, :], P("ng", l * 16 + k, 1), rb, mult, mult, tr_, bar, fh)
                th.append(part(hT[0][:, k, :], hT[1][:, k, :], h_, t, cur["bar"]))
                for m in range(2):
                    mm(pf[m][0][:, 0:4], h_[:, 128 * m:128 * m + 128], wsm[:, k, 0:4], k == 0, k == 15, t, tws, pf[m][1], fra)
                t = mm(pa[0:16, 0:256], wsm[:, k, 4:20], h_, k == 0, k == 15)
                hk.give(h_, t, th[-1])
            for m in range(2):
                t1 = tt(ft[:, 4 * m:4 * m + 4], pf[m][0][:, 0:4], P("fb", 4 * l, 4), add, t)
                PM.give(pf[m][0], t1)
            t2 = acp(aT[0:16, :], pa[0:16, 0:256], t)
            PM.give(pa, t2)

            def logsig(z, tmp, tz):
                t = af(tmp, z, ACT.Abs, tz)
                t = af(tmp, tmp, ACT.Exp, t, scale=-1.0)
                t = af(tmp, tmp, ACT.Ln, t, bias=1.0)
                return stt(z, z, 0.0, tmp, ALU.min, sub, t)
            tf = logsig(ft, fl[:, 1, :], t1)

            lam = fl[:, 2, :]
            lp = fl[:, 3, :]
            lamp = P("lam", 4 * l, 4)
            t = tt(lp[0:64, 0:2], lamp[0:64, 0:4:2], lamp[0:64, 1:4:2], mult)
            ps, fr = PM.take()
            t = mm(ps[:, 0:2], ones[0:64, :], lp[0:64, 0:2], True, True, t, fr)
            t = af(lam[:, 0:2], ps[:, 0:2], ACT.Exp, t)
            PM.give(ps, t)
            t = tt(lam[:, 2:3], lam[:, 1:2], lam[:, 0:1], sub, t)
            tlam = ts(lam[:, 3:4], lam[:, 2:3], LI, None, sub, None, t)

            qk = [[alloc(1024).rearrange("p (h t) -> p h t", h=4) for _ in range(2)] for _ in range(2)]
            vt = [alloc(1024).rearrange("p (m c) -> p m c", m=2) for _ in range(2)]
            LR = Ring([alloc(384) for _ in range(4)])
            PT = Ring([alloc(384) for _ in range(2)])
            OR = Ring([alloc(256) for _ in range(4)])
            SM = Ring([alloc(8) for _ in range(4)])
            T = {}

            def ev_copy(key, dst, scale=1.0, free=None):
                def f(ps, t):
                    T[key] = acp(dst, ps, t, free() if free else None, scale=scale)
                    return [T[key]]
                return f

            def ev_rope(key, dst, scale, nm, free):
                def f(ps, t):
                    r, fr = raw.take()
                    t0 = acp(r, ps, t, fr, scale=scale)

                    def rest():
                        yield
                        p2, fr2 = yield from grab(PM)
                        t1 = mm(p2[:, 0:256], C("permd" if nm == "d" else "permm"), r, True, True, t0, fr2)
                        t3 = ptt(r, r, C("C" + nm), mult, t0, t1, tnh)
                        yield
                        o, fo = yield from grab(OR)
                        t2 = tt(o, p2[:, 0:256], C("S" + nm), mult, t1, fo)
                        PM.give(p2, t2)
                        T[key] = tt(dst, o, r, add, t3, t2, free())
                        raw.give(r, T[key])
                        OR.give(o, T[key])
                    spawned.append(rest())
                    return [t0]
                return f

            def ev_v(key, dst, free):
                def f(ps, t):
                    r, fr = raw.take()
                    t0 = acp(r, ps, t, fr)

                    def rest():
                        yield
                        p2, fr2 = yield from grab(PM)
                        t1 = tr(p2[:, 0:128], r[:, 0:128], t0, fr2)
                        t1 = tr(p2[:, 128:256], r[:, 128:256])
                        raw.give(r, t1)
                        yield
                        T[key] = acp(dst, p2[:, 0:256].rearrange("p (m c) -> p m c", m=2), t1, free())
                        PM.give(p2, T[key])
                    spawned.append(rest())
                    return [t0]
                return f

            def ev_gate(key, dst):
                def f(ps, t):
                    t0 = af(dst, ps, ACT.Tanh, t, bar, scale=0.5)
                    T[key] = stt(dst, dst, 1.0, ps, add, mult, t0)
                    return [T[key]]
                return f

            groups = ["fox", "diff", "moba", "gla"]

            def projections():
                for gi, g in enumerate(groups):
                    b = gi % 2
                    while gi >= 2 and (groups[gi - 2], "done") not in T:
                        yield

                    def free(gi=gi):
                        return T[(groups[gi - 2], "done")] if gi >= 2 else bar
                    if g in ("fox", "diff", "moba"):
                        scs = {"fox": SC, "diff": 64 ** -0.5, "moba": SC}[g]
                        for j in range(2):
                            for h in range(4):
                                key = (g, "qk"[j], h)
                                dst = qk[b][j][:, h, :]
                                s = scs if j == 0 else 1.0
                                if g == "fox":
                                    yield from project(0, 256, hT, th, ev_copy(key, dst, s, free))
                                else:
                                    yield from project(0, 256, hT, th, ev_rope(key, dst, s, g[0], free))
                    else:
                        for j in range(2):
                            for h in range(2):
                                yield from project(0, 256, hT, th, ev_copy((g, "qk"[j], h), qk[b][j][:, h, :],
                                                                           0.125 if j == 0 else 1.0, free))
                    for h in range(4):
                        yield from project(0, 256, hT, th, ev_v((g, "v", h), vt[b][:, :, 128 * h:128 * h + 128], free))
                    for h in range(4):
                        yield from project(0, 256, hT, th, ev_gate((g, "g", h), mix[:, 4 * gi + h, :]))

            def wait(*keys):
                while not all(k in T for k in keys):
                    yield

            def softmax(ps, tps):
                L, fL = yield from grab(LR)
                sm, fs = yield from grab(SM)
                t = tt(L, ps[:, 0:384], C("mask3"), add, tps, fL)
                PM.give(ps, t)
                t = dve(lambda e: e.tensor_reduce(sm[:, 0:1], L[:, 0:128], AX.X, ALU.max, negate=True), t, fs)
                t = dve(lambda e: e.tensor_reduce(sm[:, 1:2], L[:, 128:384], AX.X, ALU.max, negate=True))
                yield
                t1 = act(lambda e: e.activation(L[:, 0:128], L[:, 0:128], ACT.Exp, bias=sm[:, 0:1], scale=1.0, accum_out=sm[:, 2:3]), t)
                t2 = act(lambda e: e.activation(L[:, 128:384], L[:, 128:384], ACT.Exp, bias=sm[:, 1:2], scale=1.0, accum_out=sm[:, 3:4]), t1)
                yield
                t3 = dve(lambda e: e.reciprocal(sm[:, 4:6], sm[:, 2:4]), t2)
                return L, sm, t3

            def finish_rms(o, to, gname, gidx):
                s, fs = yield from grab(OR)
                t = af(s, o, ACT.Square, to, fs)
                p2, t, tm = yield from rsq(s, 1, 1.0 / 128, EPS, t)
                OR.give(s, tm)
                t = stt(o, o, P(gname, gidx, 1), p2[:, 0:256], mult, mult, t)
                PM.give(p2, t)
                return t

            def pv(g, gi, h, PTt, tpt, b):
                ps, fr = yield from grab(PM)
                V = vt[b]
                mm(ps[:, 0:128], V[:, 0, 128 * h:128 * h + 128], PTt[:, 0:128], True, True, tpt, fr, T[(g, "v", h)])
                mm(ps[:, 128:256], V[:, 0, 128 * h:128 * h + 128], PTt[:, 128:256], True, False)
                t = mm(ps[:, 128:256], V[:, 1, 128 * h:128 * h + 128], PTt[:, 256:384], False, True)
                return ps, t

            def attend(gi, g):
                b = gi % 2
                q, kk_ = qk[b]
                last = []
                for h in range(4):
                    yield from wait((g, "q", h), (g, "k", h))
                    res = []
                    for sub_ in range(2 if g == "diff" else 1):
                        pr = slice(64 * sub_, 64 * sub_ + 64) if g == "diff" else slice(0, 128)
                        extra = g == "fox"
                        if extra:
                            f1, ff = yield from grab(LR)
                            ta = ts(f1[:, 0:128], C("GT"), ft[:, h:h + 1], None, mult, None, tf, ff)
                            ta = ts(f1[:, 128:384], C("G1"), ft[:, 4 + h:5 + h], None, mult, None, tf)
                        ps, fr = yield from grab(PM)
                        t = mm(ps[:, 0:128], q[pr, h, 0:128], kk_[pr, h, 0:128], True, not extra, T[(g, "q", h)], T[(g, "k", h)], fr)
                        if extra:
                            t = mm(ps[:, 0:128], C("LE"), f1[:, 0:128], False, True, ta)
                        t = mm(ps[:, 128:384], q[pr, h, 128:256], kk_[pr, h, 0:256], True, not extra)
                        if extra:
                            mm(ps[:, 128:256], ones, f1[:, 0:128], False, False)
                            t = mm(ps[:, 128:384], C("LE"), f1[:, 128:384], False, True)
                            LR.give(f1, t)
                        yield
                        res.append((yield from softmax(ps, t)))
                    yield
                    L, sm, t3 = res[0]
                    t = ts(L[:, 0:128], L[:, 0:128], sm[:, 4:5], None, mult, None, t3)
                    t = ts(L[:, 128:384], L[:, 128:384], sm[:, 5:6], None, mult, None, t3)
                    if g == "diff":
                        L2, sm2, t4 = res[1]
                        t = ts(sm2[:, 4:6], sm2[:, 4:6], lam[:, 3:4], None, mult, None, t4, tlam)
                        t = stt(L[:, 0:128], L2[:, 0:128], sm2[:, 4:5], L[:, 0:128], mult, add, t)
                        t = stt(L[:, 128:384], L2[:, 128:384], sm2[:, 5:6], L[:, 128:384], mult, add, t)
                        LR.give(L2, t)
                        SM.give(sm2, t)
                    SM.give(sm, t)
                    yield
                    ps, fr = yield from grab(PM)
                    for j in range(3):
                        t2 = tr(ps[:, 128 * j:128 * j + 128], L[:, 128 * j:128 * j + 128], t, fr)
                    LR.give(L, t2)
                    yield
                    p_, fp = yield from grab(PT)
                    t2 = acp(p_, ps[:, 0:384], t2, fp)
                    PM.give(ps, t2)
                    yield from wait((g, "v", h), (g, "g", h))
                    ps, t = yield from pv(g, gi, h, p_, t2, b)
                    PT.give(p_, t)
                    yield
                    m = mix[:, 4 * gi + h, :]
                    if g == "diff":
                        o, fo = yield from grab(OR)
                        t = acp(o, ps[:, 0:256], t, fo)
                        PM.give(ps, t)
                        yield
                        t = yield from finish_rms(o, t, "dng", l)
                        t = stt(m, o, 0.5 * (1.0 - LI), m, mult, mult, t, T[(g, "g", h)])
                        OR.give(o, t)
                    else:
                        t = stt(m, ps[:, 0:256], 0.5, m, mult, mult, t, T[(g, "g", h)])
                        PM.give(ps, t)
                    T[("mix", 4 * gi + h)] = t
                    last += [t, t2]
                    yield
                T[(g, "done")] = last + barrier()

            la = alloc(512).rearrange("p (m t) -> p m t", m=2)
            cum = alloc(512).rearrange("p (m t) -> p m t", m=2)
            ee = alloc(512).rearrange("p (m t) -> p m t", m=2)
            qe = alloc(512).rearrange("p (m t) -> p m t", m=2)
            ke = alloc(512).rearrange("p (m t) -> p m t", m=2)
            ST = alloc(1024).rearrange("p (u t) -> p u t", u=8)
            S01 = alloc(512).rearrange("p (u t) -> p u t", u=4)

            def gla():
                b = 1
                q, kk_ = qk[b]
                tz = dve(lambda e: e.memset(ST, 0.0), bar)
                ps, fr = PM.take()
                for m in range(2):
                    t = mm(ps[:, 256 * m:256 * m + 256], P("wa2", 256 * l + 128 * m, 128)[0:16, :], aT[0:16, :], True, True, t2a, fr)
                for m in range(2):
                    t = ts(la[:, m, :], ps[:, 256 * m:256 * m + 256], P("gba", 2 * l + m, 1), None, add, None, t)
                PM.give(ps, t)
                t = logsig(la, ee, t)
                t = ts(la, la, 1.0 / 16, None, mult, None, t)
                for m in range(2):
                    t = dve(lambda e, m=m: e.tensor_tensor_scan(cum[:, m, :], C("ones", 0, 1).broadcast_to([128, 256]), la[:, m, :],
                                                                0.0, mult, add), t)
                tcum = t
                yield
                yield from wait(*[("gla", j, h) for j in "qk" for h in range(2)])
                tq = [T[("gla", j, h)] for j in "qk" for h in range(2)]
                free_e = free_qk = None
                for lv in list(range(7, -2, -1)):
                    if lv >= 0:
                        w = 1 << lv
                        cv = cum.rearrange("p m (n two w) -> p (m n) two w", two=2, w=w)
                        ev = ee.rearrange("p m (n two w) -> p (m n) two w", two=2, w=w)
                        n = 512 // (2 * w)
                        ref = cv[:, :, 0, w - 1:w].broadcast_to([128, n, w])
                        t = tt(ev[:, :, 0, :], ref, cv[:, :, 0, :], sub, tcum, free_e)
                        t = tt(ev[:, :, 1, :], cv[:, :, 1, :], ref, sub)
                        t = af(ee, ee, ACT.Exp, t)
                        tq1 = tt(qe, q[:, 0:2, :], ee, mult, t, tq, free_qk)
                        tk1 = ptt(ke, kk_[:, 0:2, :], ee, mult, t, tq, free_qk)
                        free_e = [tq1, tk1]
                        qa, ka, td = qe, ke, [tq1, tk1]
                    else:
                        qa, ka, td = q[:, 0:2, :], kk_[:, 0:2, :], tq
                    yield
                    yield from need(3)
                    pe_ = [PM.take() for _ in range(2)]
                    for j in range(4 if lv < 7 else 2):
                        m, hh = (j // 2, j % 2) if lv < 7 else (0, j)
                        ks = slice(128 * m, 128 * m + 128)
                        qsl = ks if lv < 7 else slice(128, 256)
                        for e_ in range(2):
                            pr = slice(64 * e_, 64 * e_ + 64)
                            t = mm(pe_[e_][0][:, 128 * j:128 * j + 128], ka[pr, hh, ks], qa[pr, hh, qsl], True, True, td, pe_[e_][1])
                    free_qk = t
                    yield
                    for e_ in range(2):
                        ps = pe_[e_][0]
                        if lv == 7:
                            t1 = acp(S01[:, 2 * e_:2 * e_ + 2, :], ps[:, 0:256].rearrange("p (u t) -> p u t", u=2), t)
                            ts01 = t1
                        else:
                            mk = M("gla", 128 * (lv if lv >= 0 else 7), 128)
                            t1 = cpred(ST[:, 4 * e_:4 * e_ + 4, :], bc(mk, 4), ps.rearrange("p (u t) -> p u t", u=4), t, tz)
                            tst = t1
                        PM.give(ps, t1)
                    yield
                for h in range(4):
                    yield from wait(("gla", "v", h), ("gla", "g", h))
                    ps, fr = yield from grab(PM)
                    V = vt[b]
                    hs = slice(128 * h, 128 * h + 128)
                    e_, hh = h % 2, h // 2
                    mm(ps[:, 0:128], V[:, 0, hs], ST[:, 4 * e_ + hh, :], True, True, tst, ts01, fr, T[("gla", "v", h)])
                    mm(ps[:, 128:256], V[:, 0, hs], S01[:, 2 * e_ + hh, :], True, False)
                    t = mm(ps[:, 128:256], V[:, 1, hs], ST[:, 4 * e_ + 2 + hh, :], False, True)
                    o, fo = yield from grab(OR)
                    yield
                    t = acp(o, ps[:, 0:256], t, fo)
                    PM.give(ps, t)
                    yield
                    t = yield from finish_rms(o, t, "gng", l)
                    t = stt(mix[:, 12 + h, :], o, 0.5, mix[:, 12 + h, :], mult, mult, t, T[("gla", "g", h)])
                    OR.give(o, t)
                    T[("mix", 12 + h)] = t
                    yield
            t2a = t2
            run(projections(), *[attend(gi, g) for gi, g in enumerate(groups[:3])], gla(), behind=modgen)
            tm = [T[("mix", i)] for i in range(16)]
            txl = []

            def ev_res(c):
                def f(ps, t):
                    t = tt(xT[:, c, :], xT[:, c, :], ps, add, t)
                    txl.append(t)
                    return [t]
                return f
            mx = cur["acts"][0]
            pe_done = [Q.ops["t"][-1][2]]
            tm2 = []
            fill(3)
            for k in range(16):
                tm2.append(part(mx[0][:, k, :], mx[1][:, k, :], mix[:, k, :], tm[k], pe_done))
            run((x for c in range(16) for x in project(0, 256, mx, tm2, ev_res(c))), behind=modgen)
            return txl

        def store(tx):
            Q.dma(OUT, xT_[:, :], "out", tx)

        def final_norm(tx, pname):
            at[0] = 0
            bar = barrier()
            rb = alloc(256)
            sq = alloc(2048).rearrange("p (g k t) -> p g k t", g=2, k=4)
            t = norm_scale(xT, rb, sq, tx, bar)
            for k in range(16):
                t = stt(xT[:, k, :], xT[:, k, :], P(pname, k, 1), rb, mult, mult, t)
            return t

        def second(tx):
            at[0] = 0
            bar = barrier()
            A_ = mods[:, 256:304].rearrange("p (j k) -> p j k", j=3)
            hT = alloc(8192).rearrange("p (k t) -> p k t", k=16)
            ya = alloc(2048).rearrange("p (k t) -> p k t", k=8)
            rb = alloc(512)
            mark = at[0]
            cT = alloc(4096).rearrange("p (k t) -> p k t", k=16)
            sq = alloc(4096).rearrange("p (g k t) -> p g k t", g=2, k=4)
            tspill = Q.dma(XS, xT_[:, :], "spill", tx)
            tctx = Q.dma(cT, CTX.rearrange("p (k t) -> p k t", k=16), "ctx", bar)
            t = tmodl[-1]
            for j, (pn, sc0, col) in enumerate((("n1", 16, 0), ("n1", 16, 1), ("n2", 64, 0))):
                t = stt(A_[:, j, :], mod[:, sc0:sc0 + 16, col], 1.0, P(pn), add, mult, t)
            tmod = t
            sq1 = sq.rearrange("p g k t -> p (g k t)")[:, 0:2048].rearrange("p (g k t) -> p g k t", g=2, k=4)
            t = norm_scale(xT, rb[:, 0:256], sq1, tx, bar)
            t2 = norm_scale(cT, rb[:, 256:512], sq1, tctx)
            th = []
            for k in range(16):
                t = stt(hT[:, k, 0:256], xT[:, k, :], A_[:, 0, k:k + 1], rb[:, 0:256], mult, mult, t, tmod, t2)
                tb = af(hT[:, k, 0:256], hT[:, k, 0:256], ACT.Identity, t, bias=mod[:, k, 0:1])
                t = stt(hT[:, k, 256:512], cT[:, k, :], A_[:, 1, k:k + 1], rb[:, 256:512], mult, mult, t2)
                ta = af(hT[:, k, 256:512], hT[:, k, 256:512], ACT.Identity, t, bias=mod[:, k, 1:2])
                th.append([tb, ta])
            at[0] = mark
            bar = barrier()
            bar = bar + [tspill]

            mu4 = alloc(168).rearrange("p (n y) -> p n y", y=6)
            mu1 = alloc(28)
            T = {}
            tmu = tt(mu4, bcl(P("mu"), 6), bc(C("type"), 28), mult, bar)
            tmu = ts(mu1, P("mu"), -1.0, 1.0, mult, add, bar)
            tw_ = alloc(512)
            xa = alloc(512)
            sg = alloc(512).rearrange("p (m t) -> p m t", m=2)
            ab = alloc(128).rearrange("p (q n) -> p q n", q=4)
            Z = {"r": alloc(256), "k": alloc(512), "v": alloc(512)}
            zr = Ring([Z["k"], Z["v"]])

            def mixshift(dst, ps, t, n, rows, ctx_too, free, z=None):
                N = 512 if ctx_too else 256
                ring = z is None
                if ring:
                    z, fz = zr.take()
                    t = acp(z[0:rows, 0:N], ps[0:rows, 0:N], t, fz)
                t0 = t
                t1 = ts(dst[0:rows, 0:N], z[0:rows, 0:N], mu1[0:rows, n:n + 1], None, mult, None, t0, free, tmu)
                x4 = z[0:rows, 0:256].rearrange("p (r c) -> p r c", r=4)
                d4 = dst[0:rows, 0:256].rearrange("p (r c) -> p r c", r=4)

                def acc(o, i, y):
                    return stt(o, i, mu4[0:rows, n, y:y + 1], o, mult, add)
                acc(d4[:, :, 1:64], x4[:, :, 0:63], 0)
                acc(d4[:, :, 0:63], x4[:, :, 1:64], 1)
                acc(dst[0:rows, 64:256], z[0:rows, 0:192], 2)
                t1 = acc(dst[0:rows, 0:192], z[0:rows, 64:256], 3)
                if ctx_too:
                    acc(dst[0:rows, 257:512], z[0:rows, 256:511], 4)
                    t1 = acc(dst[0:rows, 256:511], z[0:rows, 257:512], 5)
                if ring:
                    zr.give(z, t1)
                return t1, t0

            def ev_w(ps, t):
                t1, t0 = mixshift(tw_, ps, t, 24, 96, True, bar)
                T["tw"] = af(tw_[0:96, :], tw_[0:96, :], ACT.Tanh, t1)
                r, fz = zr.take()
                t2 = acp(r[96:128, :], ps[96:128, :], t, fz)
                p2, fr = PM.take()
                for q_ in range(4):
                    t3 = mm(p2[:, 32 * q_:32 * q_ + 32], r[96:128, 128 * q_:128 * q_ + 128], ident[96:128, 96:128], True, True, t2, fr)
                zr.give(r, t3)
                T["ab"] = acp(ab, p2[:, 0:128].rearrange("p (q n) -> p q n", q=4), t3)
                PM.give(p2, T["ab"])
                return [t0, t2]

            def ev_a(ps, t):
                t1, t0 = mixshift(xa, ps, t, 25, 128, True, bar)
                T["xa"] = t1
                return [t0]

            def ev_g(m):
                def f(ps, t):
                    t1, t0 = mixshift(sg[:, m, :], ps, t, 26 + m, 128, False, bar)
                    t1 = af(sg[:, m, :], sg[:, m, :], ACT.Tanh, t1, scale=0.5)
                    T[("sg", m)] = ts(sg[:, m, :], sg[:, m, :], 0.5, 0.5, mult, add, t1)
                    return [t0]
                return f
            run((x for g in (project(0, 512, hT, th, ev_w), project(0, 512, hT, th, ev_a), project(0, 256, hT, th, ev_g(0)),
                             project(0, 256, hT, th, ev_g(1))) for x in g))

            def inverse(d, NA, tna, X, XT, Qs, qfree, frX):
                U = 4

                def region(buf, w, par_):
                    return buf.rearrange("p (u n two w) -> p u n two w", u=U, two=2, w=w)[:, :, :, par_, :]

                def tile4(ap, w):
                    return ap.rearrange("p (n w) -> p n w", w=w)[:, None, :, :].broadcast_to([128, U, 64 // w, w])
                t_x = dve(lambda e: e.tensor_copy(X.rearrange("p (u s) -> p u s", u=U), bc(ident, U)), frX)
                t_xt = dve(lambda e: e.tensor_copy(XT.rearrange("p (u s) -> p u s", u=U), bc(ident, U)), frX)
                tX = tXT = None
                for lv in range(7):
                    w = 1 << lv
                    mk = tile4(M("lev", (d * 7 + lv) * 64, 64), w)
                    yield from need(1)
                    ps, fr = PM.take()
                    for u in range(U):
                        sl = slice(128 * u, 128 * u + 128)
                        t = mm(ps[:, sl], NA[:, sl], ident if lv == 0 else X[:, sl], True, True, tna, fr, tX)
                    yield
                    if lv == 0:
                        tX = cpred(region(X, w, d), mk, region(ps, w, d), t, t_x)
                        PM.give(ps, tX)
                        m0 = M("xt0", d * 64, 64)[:, None, :].broadcast_to([128, U, 64])
                        xv = XT.rearrange("p (u n two) -> p u n two", u=U, two=2)[:, :, :, 1 - d]
                        nv = NA.rearrange("p (u n two) -> p u n two", u=U, two=2)[:, :, :, 1 - d]
                        tXT = cpred(xv, m0, nv, tna, t_xt)
                        continue
                    qb = Qs[lv % 2]
                    tq = cpred(region(qb, w, d), mk, region(ps, w, d), t, qfree[lv % 2])
                    PM.give(ps, tq)
                    yield from need(2)
                    if lv < 6:
                        ps, fr = PM.take()
                        for u in range(U):
                            sl = slice(128 * u, 128 * u + 128)
                            t1 = mm(ps[:, sl], XT[:, sl], qb[:, sl], True, True, tq, tXT, fr)
                    ps2, fr2 = PM.take()
                    for u in range(U):
                        sl = slice(128 * u, 128 * u + 128)
                        t2 = mm(ps2[:, sl], qb[:, sl], XT[:, sl], True, True, tq, tXT, fr2)
                    yield
                    if lv < 6:
                        tX = acp(region(X, w, d), region(ps, w, d), t1, t)
                        PM.give(ps, tX)
                    o2, i2 = region(XT, w, 1 - d), region(ps2, w, 1 - d)
                    tXT = dve(lambda e, o2=o2, i2=i2: e.tensor_copy(o2, i2), t2)
                    PM.give(ps2, tXT)
                    dq = region(qb, w, d)
                    idv = ident.rearrange("p (n two w) -> p n two w", two=2, w=w)[:, :, d, :][:, None, :, :].broadcast_to([128, U, 64 // w, w])
                    qfree[lv % 2] = pool(lambda e, dq=dq, idv=idv: e.tensor_copy(dq, idv), t2)
                    yield
                return tXT

            mark2 = at[0]
            xat = [0]

            def xbuf(n):
                a = xT_[:, xat[0]:xat[0] + n]
                xat[0] += n
                return a
            kT = xbuf(512)
            vT = xbuf(512)
            rT = alloc(256)
            kkn = alloc(512)
            rrk = alloc(256)
            Vt = alloc(512).rearrange("p (q c) -> p q c", q=4)
            lo = alloc(768).rearrange("p (j c) -> p j c", j=6)
            tmp = [xbuf(512) for _ in range(5)]
            D = []
            for d in range(2):
                kb_ = alloc(1024)
                D.append(dict(Kd=kb_[:, 0:512], Bd=kb_[:, 512:1024], X=kb_, KK=alloc(512), Rd=alloc(256), Kt=alloc(512), Bt=alloc(512),
                              NA=alloc(1024), AK=alloc(1024), RK=alloc(512), RB=alloc(512), XT=alloc(1024),
                              Q=[alloc(1024) for _ in range(2)], H=alloc(128), RU=[alloc(128) for _ in range(2)], es=alloc(8),
                              Y=xbuf(256), qf=[None, None]))
            ys = [tmp[j][:, 0:256] for j in range(3)]
            loq = [None, None]
            lot = {}

            def lload(c):
                lot[c] = Q.dma(lo, LORA[c].rearrange("p (j n) -> p j n", j=6), "lora", loq[0], bar)
            lload(0)
            tz = None
            for d in range(2):
                for nm in ("NA", "AK", "RK", "RB", "H"):
                    b_ = D[d][nm]
                    tz = dve(lambda e, b_=b_: e.memset(b_, 0.0), bar)
                for qb in D[d]["Q"]:
                    tq0 = pool(lambda e, qb=qb: e.tensor_copy(qb.rearrange("p (u s) -> p u s", u=8), bc(ident, 8)), bar)
                D[d]["qf"] = [[tq0, tq0], [tq0, tq0]]
            tyl = []

            def feed_a():
                for c in range(8):
                    for key in "rkv":
                        while c and ("zfree", key, c - 1) not in T:
                            yield
                        def f(ps, t, key=key, c=c):
                            dst = Z[key][:, 0:ps.shape[1]]
                            T[("z", key, c)] = acp(dst, ps, t, T[("zfree", key, c - 1)] if c else barrier_a)
                            return [T[("z", key, c)]]
                        yield from project(0, 256 if key == "r" else 512, hT, th, f, 3)
                    T[("z", c)] = True

            def branch_a():
                prev_done = bar
                for c in range(8):
                    E = {}

                    while ("z", c) not in T:
                        yield
                    for key, dst, n in (("r", rT, c), ("k", kT, 8 + c), ("v", vT, 16 + c)):
                        E[key], _ = mixshift(dst, None, T[("z", key, c)], n, 128, key != "r", prev_done, Z[key])
                        T[("zfree", key, c)] = E[key]
                        yield
                    tl = lot[c]
                    L6 = lo
                    t = ts(kkn, kT, P("kk", c, 1), None, mult, None, E["k"], prev_done)
                    t = af(tmp[0], kkn, ACT.Square, t, prev_done)
                    ps, t, _ = yield from rsq(tmp[0], 2, 1.0, 1e-12, t)
                    tkk = tt(kkn, kkn, ps, mult, t)
                    PM.give(ps, tkk)
                    trk = ts(rrk, rT, P("rk", c, 1), None, mult, None, E["r"], prev_done)
                    ps, fr = PM.take()
                    for q_ in range(4):
                        t = tr(ps[:, 128 * q_:128 * q_ + 128], vT[:, 128 * q_:128 * q_ + 128], E["v"], fr)
                    tV = acp(Vt, ps.rearrange("p (q c) -> p q c", q=4), t, prev_done)
                    PM.give(ps, tV)
                    psb, frb = PM.take()
                    yield

                    def prep(d):
                        G = D[d]
                        z, a_, cc, e1, e2 = tmp
                        ps, fr = PM.take()
                        t = mm(ps, L6[0:96, d, :], tw_[0:96, :], True, True, T["tw"], tl, fr)
                        t = af(z, ps, ACT.Tanh, t, twh, Q.last["v"], Q.last["p"], scale=0.5, bias=w0h[:, 8 * d + c:8 * d + c + 1])
                        PM.give(ps, t)
                        k0 = -0.5 * math.exp(-0.5)
                        tlw = ts(z, z, k0, k0, mult, add, t)
                        ps, fr = PM.take()
                        t = mm(ps, L6[:, 2 + d, :], xa, True, True, T["xa"], fr)
                        t = af(a_, ps, ACT.Tanh, t, scale=0.5, bias=a0h[:, 8 * d + c:8 * d + c + 1])
                        PM.give(ps, t)
                        ta = ts(a_, a_, 0.5, 0.5, mult, add, t)
                        yield
                        if d == 0:
                            t = dve(lambda e: e.tensor_tensor_scan(cc, C("scan"), z, 0.0, mult, add), tlw)
                        else:
                            t = dve(lambda e: e.tensor_tensor_scan(cc[:, ::-1], C("scan"), z[:, ::-1], 0.0, mult, add), tlw)
                        c4 = cc.rearrange("p (q t) -> p q t", q=4)
                        mid = 63 + d
                        end = 127 if d == 0 else 0
                        order = (2, 3, 0, 1) if d == 0 else (3, 2, 1, 0)
                        for i, q_ in enumerate(order[:3]):
                            nq = order[i + 1]
                            t = tt(G["es"][:, q_:q_ + 1], c4[:, q_, end:end + 1], c4[:, q_, mid:mid + 1], sub, t)
                            t = tt(G["es"][:, q_:q_ + 1], G["es"][:, q_:q_ + 1], c4[:, nq, mid:mid + 1], add)
                        lastq = order[3]
                        t = ts(G["es"][:, lastq:lastq + 1], G["es"][:, order[0]:order[0] + 1], 0.0, None, mult, None)
                        G["tes"] = af(G["es"][:, 0:4], G["es"][:, 0:4], ACT.Exp, t)
                        t = ts(G["es"][:, 4:8], c4[:, :, mid], 1.0, None, mult, None)
                        t = tt(c4, c4, bcl(G["es"][:, 4:8], 128), sub, t)
                        yield
                        t1 = ts(e1, a_, -1.0, P("ka", c, 1), add, mult, ta)
                        tkd = stt(e1, e1, 1.0, kT, add, mult, E["k"])
                        pr_ = G["Rd"]
                        tp_ = tt(pr_, rrk, e1[:, 0:256], mult, trk)
                        tbon = mm(psb[:, 0:256], bones, pr_, d == 0, d == 1, tp_, frb)
                        tba = tt(a_, a_, kkn, mult, tkk)
                        te = af(e2, cc, ACT.Exp, t, scale=-1.0)
                        tKd = tt(G["Kd"], e1, e2, mult, te)
                        tBd = stt(G["Bd"], a_, -1.0, e2, mult, mult)
                        yield
                        te = af(e2[:, 0:256], cc[:, 0:256], ACT.Exp, tBd)
                        tRd = tt(G["Rd"], rT, e2[:, 0:256], mult, te, tbon, E["r"])
                        t = tt(cc, cc, z, sub, te)
                        te = af(e2, cc, ACT.Exp, t, tRd)
                        tKK = tt(G["KK"], kkn, e2, mult, te)
                        return tbon, [tKd, tBd, tRd, tKK]

                    def scores(d, tin):
                        G = D[d]
                        sm = M("strict", 128 * d, 128)
                        im = M("incl", 128 * d, 128)
                        for nm, src in (("Kt", "Kd"), ("Bt", "Bd")):
                            ps, fr = PM.take()
                            for q_ in range(4):
                                t = tr(ps[:, 128 * q_:128 * q_ + 128], G[src][:, 128 * q_:128 * q_ + 128], tin, fr)
                            G["t" + nm] = acp(G[nm], ps, t)
                            PM.give(ps, G["t" + nm])
                        for nm, src in (("NA", "Bd"), ("AK", "Kd")):
                            pe_ = [PM.take() for _ in range(2)]
                            for q_ in range(4):
                                sl = slice(128 * q_, 128 * q_ + 128)
                                for e_ in range(2):
                                    pr = slice(64 * e_, 64 * e_ + 64)
                                    t1 = mm(pe_[e_][0][:, sl], G[src][pr, sl], G["KK"][pr, sl], True, True, tin, pe_[e_][1])
                            for e_ in range(2):
                                ps = pe_[e_][0]
                                t = cpred(G[nm][:, 512 * e_:512 * e_ + 512].rearrange("p (u t) -> p u t", u=4), bc(sm, 4),
                                          ps.rearrange("p (u t) -> p u t", u=4), t1, tz)
                                PM.give(ps, t)
                            G["t" + nm] = t
                            yield
                        pe_ = [PM.take() for _ in range(2)]
                        for j, src in enumerate(("Bd", "Kd")):
                            for q_ in range(2):
                                sl = slice(128 * q_, 128 * q_ + 128)
                                for e_ in range(2):
                                    pr = slice(64 * e_, 64 * e_ + 64)
                                    o = 256 * j + 128 * q_
                                    t1 = mm(pe_[e_][0][:, o:o + 128], G[src][pr, sl], G["Rd"][pr, sl], True, True, tin, pe_[e_][1])
                        for e_ in range(2):
                            ps = pe_[e_][0]
                            for j, nm in enumerate(("RB", "RK")):
                                t = cpred(G[nm][:, 256 * e_:256 * e_ + 256].rearrange("p (u t) -> p u t", u=2), bc(im, 2),
                                          ps[:, 256 * j:256 * j + 256].rearrange("p (u t) -> p u t", u=2), t1, tz)
                                G["t" + nm] = t
                            PM.give(ps, t)
                        G["tsc"] = t1
                        yield

                    def chain(d):
                        G = D[d]
                        order = (2, 3, 0, 1) if d == 0 else (3, 2, 1, 0)
                        H = G["H"]
                        R_, U_ = G["RU"]
                        tH = [dve(lambda e: e.memset(H, 0.0))]
                        for i, q_ in enumerate(order):
                            sl = slice(128 * q_, 128 * q_ + 128)
                            ps, fr = PM.take()
                            mm(ps[:, 0:128], G["KK"][:, sl], H, True, False, tH, fr, G["tAK"])
                            for e_ in range(2):
                                t = mm(ps[:, 64 * e_:64 * e_ + 64], G["AK"][:, 512 * e_ + 128 * q_:512 * e_ + 128 * q_ + 128],
                                       Vt[:, q_, 64 * e_:64 * e_ + 64], False, e_ == 1, tV)
                            t = acp(R_, ps[:, 0:128], t)
                            yield
                            for e_ in range(2):
                                t2 = mm(ps[:, 128 + 64 * e_:192 + 64 * e_], G["XT"][:, 512 * e_ + 128 * q_:512 * e_ + 128 * q_ + 128],
                                        R_[:, 64 * e_:64 * e_ + 64], True, True, t, G["tinv"])
                            t2 = acp(U_, ps[:, 128:256], t2)
                            PM.give(ps, t2)
                            yield
                            if q_ < 2:
                                ps, fr = PM.take()
                                mm(ps[:, 0:128], H, G["Rd"][:, sl], True, False, t2, fr, G["tRK"], G["tRB"])
                                for e_ in range(2):
                                    o = ps[64 * e_:64 * e_ + 64, 0:128]
                                    ua = slice(256 * e_ + 128 * q_, 256 * e_ + 128 * q_ + 128)
                                    mm(o, Vt[:, q_, 64 * e_:64 * e_ + 64], G["RK"][:, ua], False, False)
                                    t3 = mm(o, U_[:, 64 * e_:64 * e_ + 64], G["RB"][:, ua], False, True)
                                ty = acp(G["Y"][:, sl], ps[:, 0:128], t3)
                                PM.give(ps, ty)
                                G["tY"] = ty
                            if i < 3:
                                ps, fr = PM.take()
                                mm(ps[:, 0:128], ident, H, True, False, fr, tH)
                                mm(ps[:, 0:128], G["Kt"][:, sl], Vt[:, q_, :], False, False, G["tKt"])
                                t4 = mm(ps[:, 0:128], G["Bt"][:, sl], U_, False, True, t2, G["tBt"])
                                tH = [acp(H[64 * e_:64 * e_ + 64, 64 * e_:64 * e_ + 64], ps[64 * e_:64 * e_ + 64, 64 * e_:64 * e_ + 64], t4, G["tes"],
                                          scale=G["es"][64 * e_:64 * e_ + 64, q_:q_ + 1]) for e_ in range(2)]
                                PM.give(ps, *tH)
                            yield

                    def whole(d, tin):
                        yield from scores(d, tin)
                        G = D[d]
                        hs = [slice(0, 512), slice(512, 1024)]
                        G["tinv"] = yield from together(*[inverse(d, G["NA"][:, hs[e_]], G["tNA"], G["X"][:, hs[e_]], G["XT"][:, hs[e_]],
                                                                  [x[:, hs[e_]] for x in G["Q"]], G["qf"][e_], [prev_done, G["tsc"]])
                                                          for e_ in range(2)])
                        yield from chain(d)
                    b0, ti0 = yield from prep(0)
                    b1, ti1 = yield from prep(1)
                    yield from together(whole(0, ti0), whole(1, ti1))
                    y, s_ = ys[0:2]
                    t = tt(y, D[0]["Y"], D[1]["Y"], add, D[0]["tY"], D[1]["tY"])
                    ps, fr = PM.take()
                    t1 = mm(ps[:, 0:256], bones, y, True, True, t, fr)
                    t = stt(y, ps[:, 0:256], -1.0 / 64, y, mult, add, t1)
                    t1 = af(s_, y, ACT.Square, t)
                    PM.give(ps, t)
                    ps, t, _ = yield from rsq(s_, 2, 1.0 / 64, 64e-5, t1)
                    t = tt(y, y, ps[:, 0:256], mult, t)
                    PM.give(ps, t)
                    t = ts(y, y, P("lnw", c, 1), P("lnb", c, 1), mult, add)
                    t = tt(s_, psb[:, 0:256], vT[:, 0:256], mult, b1)
                    PM.give(psb, t)
                    t = tt(y, y, s_, add)
                    ps, fr = PM.take()
                    for m in range(2):
                        t1 = mm(ps[:, 0:256], L6[:, 4 + m, :], sg[:, m, :], m == 0, m == 1, fr, T[("sg", 0)], T[("sg", 1)], tl)
                    t = tt(ya[:, c, :], y, ps[:, 0:256], mult, t, t1)
                    PM.give(ps, t)
                    loq[0] = t
                    if c < 7:
                        lload(c + 1)
                    tyl.append(t)
                    prev_done = barrier()
                    yield
            w0h = alloc(16)
            a0h = alloc(16)
            ts(w0h, P("w0"), 0.5, None, mult, None, bar)
            twh = ts(a0h, P("a0"), 0.5, None, mult, None, bar)
            barrier_a = barrier()
            run(branch_a(), feed_a())
            if upto == 3:
                for c in range(8):
                    t = acp(xT[:, c, :], ya[:, c, :], tyl)
                return [t]

            at[0] = mark2
            bar = barrier()
            yb = alloc(2048).rearrange("p (k t) -> p k t", k=8)
            mark3 = at[0]
            gb = {k: alloc(64).rearrange("p (q n) -> p q n", q=4) for k in ("g", "beta", "nbeta", "gc", "egc", "negc", "gt", "egt", "eend", "tmp", "tmp2")}
            ea = alloc(16)
            t = af(ea, P("alog"), ACT.Exp, bar)
            tea = t
            av = ab[:, :, 0:16]
            bv = ab[:, :, 16:32]
            t = tt(gb["g"], av, bc(P("dtb"), 4), add, T["ab"], bar)
            t = af(gb["tmp"], gb["g"], ACT.Abs, t)
            t = af(gb["tmp"], gb["tmp"], ACT.Exp, t, scale=-1.0)
            t = af(gb["tmp"], gb["tmp"], ACT.Ln, t, bias=1.0)
            t = stt(gb["g"], gb["g"], 0.0, gb["tmp"], ALU.max, add, t)
            t = stt(gb["g"], gb["g"], -1.0, bc(ea, 4), mult, mult, t, tea)
            tg = t
            t = af(gb["beta"], bv, ACT.Tanh, T["ab"], bar, scale=0.5)
            t = ts(gb["beta"], gb["beta"], 0.5, 0.5, mult, add, t)
            tbeta = ts(gb["nbeta"], gb["beta"], -1.0, None, mult, None, t)
            ps, fr = PM.take()
            p3 = ps[:, 0:64].rearrange("p (q n) -> p q n", q=4)
            p4_ = ps[:, 64:128].rearrange("p (q n) -> p q n", q=4)
            for d in range(2):
                for q_ in range(4):
                    t = mm(p3[:, q_, 8 * d:8 * d + 8], C("LE" if d == 0 else "GE"), gb["g"][:, q_, 8 * d:8 * d + 8], True, True, tg, fr)
            for q_ in range(4):
                t = mm(p4_[:, q_, :], ones, gb["g"][:, q_, :], True, True)
            t1 = af(gb["egc"], p3, ACT.Exp, t)
            t = acp(gb["gc"], p3, t)
            t = tt(gb["gt"], p4_, gb["gc"], sub, t)
            t1 = af(gb["eend"], gb["gt"], ACT.Exp, t)
            t1 = af(gb["egt"], p4_, ACT.Exp, t)
            PM.give(ps, t1)
            tgb = ts(gb["negc"], gb["egc"], -1.0, None, mult, None, t1)

            xat[0] = 0
            Y_ = {"q": xbuf(256), "k": xbuf(512), "v": xbuf(512), "z": xbuf(256)}
            HB = []
            for d in range(2):
                HB.append(dict(NA=alloc(512), AT=alloc(256), X=alloc(512), XT=alloc(512), Q=[alloc(512) for _ in range(2)],
                               S=alloc(128), RU=[alloc(128) for _ in range(2)], dec=alloc(512), gl=alloc(512),
                               qs=alloc(256), Ke=alloc(512), O=alloc(256), qf=[None, None]))
            kb = alloc(512)
            vb = alloc(512)
            qb_ = alloc(256)
            gzb = alloc(256)
            kt_ = alloc(512)
            vt_ = alloc(512)
            t1b = alloc(512)
            t2b = alloc(512)
            for d in range(2):
                for qb in HB[d]["Q"]:
                    tq0 = pool(lambda e, qb=qb: e.tensor_copy(qb.rearrange("p (u s) -> p u s", u=4), bc(ident, 4)), bar)
                HB[d]["qf"] = [tq0, tq0]
            tyb = []

            def feed_b():
                for h in range(8):
                    for key in "qkvz":
                        while h and ("yfree", key, h - 1) not in T:
                            yield
                        def f(ps, t, key=key, h=h):
                            T[("y", key, h)] = acp(Y_[key], ps, t, T[("yfree", key, h - 1)] if h else bar)
                            return [T[("y", key, h)]]
                        yield from project(0, 256 if key in "qz" else 512, hT, th, f, 1)
                    T[("y", h)] = True

            def branch_b():
                prev = bar
                for h in range(8):
                    E = {}

                    while ("y", h) not in T:
                        yield
                    for key, dst, n in (("q", qb_, h), ("k", kb, 8 + h), ("v", vb, 16 + h)):
                        N = 256 if key == "q" else 512
                        z = Y_[key]
                        zv = z.rearrange("p (s t) -> p s t", t=256)
                        w_ = t1b[:, 0:N]
                        wv = w_.rearrange("p (s t) -> p s t", t=256)
                        ts(w_, z, P("conv", 24 + n, 1), None, mult, None, T[("y", key, h)], prev)
                        stt(wv[:, :, 1:256], zv[:, :, 0:255], P("conv", n, 1), wv[:, :, 1:256], mult, add)
                        t1 = stt(wv[:, :, 0:255], zv[:, :, 1:256], P("conv", 48 + n, 1), wv[:, :, 0:255], mult, add)
                        t2 = af(t2b[:, 0:N], w_, ACT.Tanh, t1, prev, scale=0.5)
                        E[key] = stt(dst, t2b[:, 0:N], 1.0, w_, add, mult, t2, prev)
                        T[("yfree", key, h)] = t1
                        yield
                    t0 = af(gzb, Y_["z"], ACT.Tanh, T[("y", "z", h)], prev, scale=0.5)
                    E["gz"] = stt(gzb, gzb, 1.0, Y_["z"], add, mult, t0)
                    T[("yfree", "z", h)] = E["gz"]
                    tsq = None
                    for buf, N, fac, key in ((qb_, 256, 0.5 * 128 ** -0.5, "q"), (kb, 512, 0.5, "k")):
                        t = af(t2b[:, 0:N], buf, ACT.Square, E[key], E["v"], tsq)
                        ps, t, tsq = yield from rsq(t2b[:, 0:N], 1, 0.25, 1e-12, t)
                        E[key] = stt(buf, buf, fac, ps[:, 0:N], mult, mult, t)
                        PM.give(ps, E[key])
                    for src, dst, key, sc0 in ((kb, kt_, "kt", 1.0), (vb, vt_, "vt", 0.5)):
                        ps, fr = PM.take()
                        for q_ in range(4):
                            t = tr(ps[:, 128 * q_:128 * q_ + 128], src[:, 128 * q_:128 * q_ + 128], E["k"], E["v"], fr)
                        E[key] = acp(dst, ps, t, prev, scale=sc0)
                        PM.give(ps, E[key])
                    yield

                    def whole(d):
                        G = HB[d]
                        col = 8 * d + h
                        a_m, b_m = ("GT", "LE") if d == 0 else ("LT", "GE")
                        for q_ in range(4):
                            t = ts(G["gl"][:, 128 * q_:128 * q_ + 128], C(a_m), gb["g"][:, q_, col:col + 1], None, mult, None, prev)
                        ps, fr = PM.take()
                        for q_ in range(4):
                            t1 = mm(ps[:, 128 * q_:128 * q_ + 128], G["gl"][:, 128 * q_:128 * q_ + 128], C(b_m), True, True, t, fr)
                        td = af(G["dec"], ps, ACT.Exp, t1, prev)
                        PM.give(ps, td)
                        yield
                        for q_ in range(4):
                            sl = slice(128 * q_, 128 * q_ + 128)
                            tke = acp(G["Ke"][:, sl], kt_[:, sl], E["kt"], prev, tgb, scale=gb["eend"][:, q_, col:col + 1])
                        tds = ptt(G["gl"].rearrange("p (u t) -> p u t", u=4), G["dec"].rearrange("p (u t) -> p u t", u=4),
                                  bc(C("strict", 128 * d, 128), 4), mult, td, t1)
                        ps, fr = PM.take()
                        for q_ in range(4):
                            sl = slice(128 * q_, 128 * q_ + 128)
                            t1 = mm(ps[:, sl], kb[:, sl], kb[:, sl], True, True, E["k"], fr)
                        for q_ in range(4):
                            sl = slice(128 * q_, 128 * q_ + 128)
                            t1 = stt(G["NA"][:, sl], G["gl"][:, sl], gb["nbeta"][:, q_, col:col + 1], ps[:, sl], mult, mult, tds, t1, tbeta)
                        PM.give(ps, t1)
                        tNA = t1
                        yield
                        ps, fr = PM.take()
                        for q_ in range(2):
                            sl = slice(128 * q_, 128 * q_ + 128)
                            t1 = mm(ps[:, sl], kb[:, sl], qb_[:, sl], True, True, E["q"], fr)
                        for q_ in range(2):
                            t2 = mm(ps[:, 256 + 128 * q_:384 + 128 * q_], gb["g"][:, q_, col:col + 1].broadcast_to([128, 128]), C(b_m), True, True)
                        tdi = ptt(G["dec"][:, 0:256].rearrange("p (u t) -> p u t", u=2), G["dec"][:, 0:256].rearrange("p (u t) -> p u t", u=2),
                                  bc(C("incl", 128 * d, 128), 2), mult, tds)
                        tat = tt(G["AT"], G["dec"][:, 0:256], ps[:, 0:256], mult, t2, tdi, prev)
                        te = af(G["qs"], ps[:, 256:512], ACT.Exp, t2, prev, tat)
                        PM.give(ps, tat, te)
                        tqs = tt(G["qs"], G["qs"], qb_, mult, te)
                        yield
                        tinv = yield from inverse(d, G["NA"], tNA, G["X"], G["XT"], G["Q"], G["qf"], prev)
                        order = (2, 3, 0, 1) if d == 0 else (3, 2, 1, 0)
                        S = G["S"]
                        R_, U_ = G["RU"]
                        tS = dve(lambda e: e.memset(S, 0.0), prev)
                        for i, q_ in enumerate(order):
                            sl = slice(128 * q_, 128 * q_ + 128)
                            ps, fr = PM.take()
                            t = mm(ps[:, 0:128], kb[:, sl], S, True, True, tS, fr)
                            t = stt(R_, ps[:, 0:128], gb["negc"][:, q_, col:col + 1], vt_[:, sl], mult, add, t, E["vt"], tgb)
                            yield
                            t = mm(ps[:, 128:256], G["XT"][:, sl], R_, True, True, t, tinv)
                            tU = acp(U_, ps[:, 128:256], t, scale=gb["beta"][:, q_, col:col + 1])
                            PM.give(ps, tU)
                            yield
                            if q_ < 2:
                                ps, fr = PM.take()
                                mm(ps[:, 0:128], S, G["qs"][:, sl], True, False, tqs, tU, fr)
                                t = mm(ps[:, 0:128], U_, G["AT"][:, sl], False, True, tat)
                                G["tO"] = acp(G["O"][:, sl], ps[:, 0:128], t)
                                PM.give(ps, G["tO"])
                            if i < 3:
                                ps, fr = PM.take()
                                t = mm(ps[:, 0:128], G["Ke"][:, sl], U_, True, True, tke, tU, fr)
                                tS = stt(S, S, gb["egt"][:, q_, col:col + 1], ps[:, 0:128], mult, add, t)
                                PM.give(ps, tS)
                            yield
                    yield from together(whole(0), whole(1))
                    y = HB[0]["O"]
                    t = tt(y, y, HB[1]["O"], add, HB[0]["tO"], HB[1]["tO"])
                    t = af(t2b[:, 0:256], y, ACT.Square, t)
                    ps, t, _ = yield from rsq(t2b[:, 0:256], 1, 1.0 / 128, EPS, t)
                    t = stt(y, y, P("gnw"), ps[:, 0:256], mult, mult, t)
                    PM.give(ps, t)
                    t = stt(yb[:, h, :], y, 0.5, gzb, mult, mult, t, E["gz"])
                    tyb.append(t)
                    prev = barrier()
                    yield
            run(branch_b(), feed_b())
            if upto == 4:
                for c in range(8):
                    t = acp(xT[:, c, :], yb[:, c, :], tyb)
                return [t]

            scope("c", 3, 1)
            at[0] = mark3
            bar = barrier()
            ahead["end"] = nb1 + 28 + 32 + 48 + 16
            xs_ = cur["acts"][0]
            fill(2)
            tback = Q.dma(xT_[:, :], XS, "back", bar)
            tx2 = [part(xs_[0][:, k, :], xs_[1][:, k, :], hT[:, k, 0:256], bar) for k in range(16)]
            mg = alloc(4096).rearrange("p (k t) -> p k t", k=16)
            ga = Ring([alloc(256) for _ in range(2)])
            gbb = Ring([alloc(256) for _ in range(2)])
            tmg = []

            def merges():
                for c in range(16):
                    E = {}
                    for nm, ring in (("a", ga), ("b", gbb)):
                        buf, fb_ = ring.take()

                        def f(ps, t, buf=buf, fb_=fb_, nm=nm):
                            t0 = af(buf, ps, ACT.Tanh, t, fb_, bar, scale=0.5)
                            E[nm] = t0
                            E[nm + "b"] = buf
                            return [t0]
                        yield from project(0, 256, xs_, tx2, f)
                    fill(1)
                    w, tw, s = ready.popleft()
                    fill(2)
                    ps, fr = PJ.take()
                    for k in range(8):
                        t = mm(ps[:, 0:256], w[:, k, :], ya[:, k, :], k == 0, k == 7, tw, fr, tyl)
                    for k in range(8):
                        t = mm(ps[:, 256:512], w[:, 8 + k, :], yb[:, k, :], k == 0, k == 7, tyb)
                    wgive(s, t)
                    t1 = stt(E["ab"], E["ab"], 1.0, ps[:, 0:256], add, mult, t, E["a"])
                    t2 = stt(E["bb"], E["bb"], 1.0, ps[:, 256:512], add, mult, E["b"])
                    PJ.give(ps, t2)
                    t3 = tt(mg[:, c, :], E["ab"], E["bb"], add, bar)
                    ga.give(E["ab"], t3)
                    gbb.give(E["bb"], t3)
                    tmg.append(t3)
                    yield
            run(merges())
            g1h = alloc(16)
            tgh = ts(g1h, mod[:, 32:48, 0], 0.5, None, mult, None, bar)
            txl = []

            def ev_x(c, gate):
                def f(ps, t):
                    t = stt(xT[:, c, :], ps, gate, xT[:, c, :], mult, add, t, tgh, tback)
                    txl.append(t)
                    return [t]
                return f
            pe_done = [Q.ops["t"][-1][2]]
            pe_done[0].need = True
            fill(3)
            tm2 = [part(xs_[0][:, k, :], xs_[1][:, k, :], mg[:, k, :], tmg[k], pe_done) for k in range(16)]
            run((x for c in range(16) for x in project(0, 256, xs_, tm2, ev_x(c, g1h[:, c:c + 1]))))

            scope("m", 4, 2)
            at[0] = 0
            bar = barrier()
            ahead["end"] = NT - NMOD
            h2, us = cur["acts"]
            sq = alloc(2048).rearrange("p (g k t) -> p g k t", g=2, k=4)
            rb = alloc(256)
            tr3 = Ring([alloc(256) for _ in range(3)])
            t = norm_scale(xT, rb, sq, txl, bar)
            fill(2)
            th2 = []
            for k in range(16):
                h_, fh = tr3.take()
                t = stt(h_, xT[:, k, :], A_[:, 2, k:k + 1], rb, mult, mult, t, fh)
                t = af(h_, h_, ACT.Identity, t, bias=mod[:, 48 + k, 0:1])
                th2.append(part(h2[0][:, k, :], h2[1][:, k, :], h_, t))
                tr3.give(h_, th2[-1])
            txn = []
            for g in range(4):
                tu = []

                def ev_u(k):
                    def f(ps, t):
                        h_, fh = tr3.take()
                        t0 = af(h_, ps, ACT.Relu, t, fh)
                        t1 = tt(h_, h_, h_, mult, t0)
                        tu.append(part(us[0][:, k, :], us[1][:, k, :], h_, t1, last_pe))
                        tr3.give(h_, tu[-1])
                        return [t0]
                    return f
                last_pe = [Q.ops["t"][-1][2]]
                run((x for k in range(16) for x in project(0, 256, h2, th2, ev_u(k))))

                def ev_o(c):
                    def f(ps, t):
                        txn.append(stt(xT[:, c, :], ps, mod[:, 80 + c, 0:1], xT[:, c, :], mult, add, t, th2))
                        return [txn[-1]]
                    return f
                run((x for c in range(16) for x in project(0, 256, us, tu, ev_o(c))))
            return txn

        t = [tx, tnh]
        scope("a", 3, 1, 4)
        if upto >= 1:
            t = layer(0, t)
        if upto >= 2:
            t = layer(1, t)
            t = final_norm(t, "fng")
        if upto >= 3:
            for _ in modgen:
                pass
            scope("b", 0, 0)
            t = second(t)
        if upto >= 5:
            t = final_norm(t, "fnw")
        store(t)

        totals = Q.number()
        sem = {s: ctx.enter_context(nc.semaphore("s_" + s)) for s in totals}
        block = ctx.enter_context(nc.Block())

        @block.sync
        def _(e):
            Q.play("s", e, sem, totals)

        @block.tensor
        def _(e):
            Q.play("t", e, sem, totals)

        @block.vector
        def _(e):
            Q.play("v", e, sem, totals)

        @block.scalar
        def _(e):
            Q.play("a", e, sem, totals)

        @block.gpsimd
        def _(e):
            Q.play("p", e, sem, totals)


SEG = {}


def _segments():
    o = 0
    for n, w in (("fq", 512), ("fk", 512), ("fv", 512), ("ff", 4), ("fg", 512), ("dq", 512), ("dk", 512), ("dv", 512),
                 ("dg", 512), ("mq", 512), ("mk", 512), ("mv", 512), ("mg", 512), ("gq", 256), ("gk", 256), ("gv", 512),
                 ("ga", 16), ("gg", 512)):
        SEG[n] = (o, w)
        o += w


_segments()


def layout(inp):
    g = {k: np.asarray(v) for k, v in inp.items()}
    W = np.empty((NT, 128, 16, 128), np.float32)
    n = [0]

    def tiles(w):
        m = w.shape[1] // 128
        W[n[0]:n[0] + m] = w.reshape(16, 128, m, 128).transpose(2, 1, 0, 3)
        n[0] += m

    wsm = np.empty((2, 128, 320), np.float32)
    for l in range(2):
        w = g["w_in"][l]
        for nm in ("fq", "fk", "fv", "fg", "dq", "dk", "dv", "dg", "mq", "mk", "mv", "mg", "gq", "gk", "gv", "gg"):
            o, wd = SEG[nm]
            tiles(w[:, o:o + wd])
        sm = np.concatenate([w[:, SEG["ff"][0]:SEG["ff"][0] + 4], w[:, SEG["ga"][0]:SEG["ga"][0] + 16]], 1)
        wsm[l] = sm.reshape(16, 128, 20).transpose(1, 0, 2).reshape(128, 320)
        tiles(g["w_out"][l])
    W[n[0]:n[0] + NMOD] = g["mod_w_2"][0].reshape(4, 4, 128, 24, 512).transpose(3, 0, 2, 1, 4).reshape(NMOD, 128, 16, 128)
    n[0] += NMOD
    w = g["in_w_2"][0]
    AC = 3552
    tiles(np.concatenate([w[:, 3072:3168], w[:, AC + 4096:AC + 4128]], 1))
    tiles(w[:, 3168:3296])
    tiles(w[:, 3296:3552])
    for c in range(8):
        for j in range(3):
            tiles(w[:, 1024 * j + 128 * c:1024 * j + 128 * c + 128])
    for c in range(8):
        for j in range(4):
            tiles(w[:, AC + 1024 * j + 128 * c:AC + 1024 * j + 128 * c + 128])
    G0 = AC + 4128
    ua, ub = g["up_a_2"][0], g["up_b_2"][0]
    uab = np.concatenate([ua, ub], 0)
    for c in range(16):
        tiles(w[:, G0 + 128 * c:G0 + 128 * c + 128])
        tiles(w[:, G0 + 2048 + 128 * c:G0 + 2048 + 128 * c + 128])
        tiles(uab[:, 128 * c:128 * c + 128])
    tiles(g["out_w_2"][0])
    for q in range(4):
        tiles(g["mlp_w1_2"][0][:, 2048 * q:2048 * q + 2048])
        tiles(g["mlp_w2_2"][0][2048 * q:2048 * q + 2048])
    assert n[0] == NT, (n[0], NT)

    par = np.zeros((128, PARN), np.float32)

    def put(name, v, i=0):
        o = PAR[name][0] + i
        par[:v.shape[0], o:o + v.shape[1]] = v

    def col(v):
        return v.reshape(-1, 128).T

    def rep(v):
        return np.broadcast_to(v.reshape(1, -1), (128, v.size))
    for l in range(2):
        put("ng", col(g["norm_g"][l]), 16 * l)
        put("fb", rep(g["fox_fb"][l]), 4 * l)
        put("lam", g["diff_lam"][l].T, 4 * l)
        put("dng", col(g["diff_norm_g"][l]), l)
        put("gng", col(g["gla_norm_g"][l]), l)
        put("gba", col(g["gla_ba"][l]), 2 * l)
        put("wa2", g["gla_wa2"][l], 256 * l)
    put("fng", col(g["final_norm_g"]))
    cc = np.stack([col(g["c_2"][0]), col(g["c_ctx_2"])], 2)
    put("c", cc.reshape(128, 32))
    put("modb", col(g["mod_b_2"][0]))
    put("n1", col(g["norm1_w_2"][0]))
    put("n2", col(g["norm2_w_2"][0]))
    mu = g["rwkv_mu_2"][0]
    put("mu", col(mu[0:3072]))
    put("mu", mu[3072:3168].reshape(96, 1), 24)
    put("mu", col(mu[3168:3552]), 25)
    for d in range(2):
        put("w0", col(g["rwkv_w0_2"][0, d]), 8 * d)
        put("a0", col(g["rwkv_a0_2"][0, d]), 8 * d)
    put("kk", col(g["rwkv_k_k_2"][0]))
    put("ka", col(g["rwkv_k_a_2"][0]))
    put("rk", col(g["rwkv_r_k_2"][0].reshape(-1)))
    put("lnw", col(g["rwkv_ln_w_2"][0]))
    put("lnb", col(g["rwkv_ln_b_2"][0]))
    for k in range(3):
        put("conv", col(g["gdn_conv_w_2"][0, k]), 24 * k)
    put("alog", rep(g["gdn_a_log_2"][0]))
    put("dtb", rep(g["gdn_dt_bias_2"][0]))
    put("gnw", col(g["gdn_norm_w_2"][0]))
    put("fnw", col(g["final_norm_w_2"]))

    lora = np.zeros((8, 128, 6, 128), np.float32)
    for c in range(8):
        cs = slice(128 * c, 128 * c + 128)
        for d in range(2):
            lora[c, 0:96, d] = g["rwkv_w_up_2"][0, d][:, cs]
            lora[c, :, 2 + d] = g["rwkv_a_up_2"][0, d][:, cs]
            lora[c, :, 4 + d] = g["rwkv_g_up_2"][0][128 * d:128 * d + 128, cs]

    def chan(v):
        return np.ascontiguousarray(v[0].T.reshape(16, 128, 256).transpose(1, 0, 2).reshape(128, 4096))
    cst, mk = constants()
    return {"w": W.reshape(NT, 128, 2048), "wsm": wsm, "lora": lora.reshape(8, 128, 768), "par": par, "cst": cst, "msk": mk.view(np.uint32),
            "ctx": chan(g["ctx_2"]), "x": chan(g["x"])}


def build(nc, arrays, upto=99):
    aps = {}
    for k, v in arrays.items():
        aps[k] = nc.dram_tensor("in_" + k, v.shape, mybir.dt.from_np(v.dtype), kind="ExternalInput").ap()
    out = nc.dram_tensor("out_0", (128, 4096), F32, kind="ExternalOutput").ap()
    xs = nc.dram_tensor("x_kept", (128, 4096), F32, kind="Internal").ap()
    program(nc, aps["w"], aps["wsm"], aps["lora"], aps["par"], aps["cst"], aps["msk"], aps["ctx"], aps["x"], xs, out, upto)


def kernel(**inputs):
    import concourse.bacc as _bacc
    from concourse.bass_utils import run_bass_kernel_spmd as _run

    nc = _bacc.Bacc("TRN2", target_bir_lowering=False, num_devices=1)
    arrays = layout(inputs)
    build(nc, arrays)
    r = _run(nc, [{"in_" + k: v for k, v in arrays.items()}], core_ids=[0])
    o = r.results[0]["out_0"]
    return o.reshape(128, 16, 256).transpose(2, 1, 0).reshape(1, 256, 2048)
```
